# Optimizing a Trainium2 kernel written in Bass

```python
import math
import jax, jax.numpy as jnp
from jax import lax
import numpy as np

D_MODEL = 1024
BATCH = 1
SEQ = 512
DEPTH = 2
DEC_BATCH = 1
DEC_SEQ = 512
PAST_LEN = 128

N_META = 16
N_MIXERS = 2
N_ATTN_LAYERS = (DEPTH + 1) // 2
N_SSD_LAYERS = DEPTH // 2
EPS = 1e-6
MLA_HEADS = 16
QK_NOPE_DIM = 64
QK_ROPE_DIM = 32
QK_HEAD_DIM = QK_NOPE_DIM + QK_ROPE_DIM
V_HEAD_DIM = 64
Q_LORA_RANK = 384
KV_LORA_RANK = 256
ROPE_BASE = 10000.0
Q_BLOCK = 128
D_INNER = 2 * D_MODEL
SSD_HEAD_DIM = 64
SSD_HEADS = D_INNER // SSD_HEAD_DIM
SSD_GROUPS = 4
HEADS_PER_GROUP = SSD_HEADS // SSD_GROUPS
D_STATE = 128
D_CONV = 5
CONV_DIM = D_INNER + 2 * SSD_GROUPS * D_STATE
CHUNK = 128
META_PAD = CHUNK - N_META
FFN_HIDDEN = -(-8 * D_MODEL // (3 * 256)) * 256

kernel_name = 'hybrid_mla_ssd_encoder'

def rmsnorm(x, w):
    xf = x.astype(jnp.float32)
    y = xf * lax.rsqrt(jnp.mean(xf * xf, axis=-1, keepdims=True) + EPS) * w.astype(jnp.float32)
    return y.astype(x.dtype)

def apply_rope(x, pos):
    x_pass, x_rot = jnp.split(x, [QK_NOPE_DIM], axis=-1)
    half = QK_ROPE_DIM // 2
    inv_freq = ROPE_BASE ** (-jnp.arange(half, dtype=jnp.float32) / half)
    ang = pos[:, None] * inv_freq[None, :]
    cos = jnp.cos(ang)[None, :, None, :]
    sin = jnp.sin(ang)[None, :, None, :]
    xr = x_rot.astype(jnp.float32)
    x1, x2 = xr[..., :half], xr[..., half:]
    rot = jnp.concatenate([x1 * cos - x2 * sin, x1 * sin + x2 * cos], axis=-1)
    return jnp.concatenate([x_pass, rot.astype(x.dtype)], axis=-1)

def block_attention(q, k, v):
    b, L, H, dq = q.shape
    nb = -(-L // Q_BLOCK)
    pad = nb * Q_BLOCK - L
    qp = jnp.pad(q, ((0, 0), (0, pad), (0, 0), (0, 0)))
    qp = jnp.moveaxis(qp.reshape(b, nb, Q_BLOCK, H, dq), 1, 0)
    scale = 1.0 / math.sqrt(QK_HEAD_DIM)

    def one_block(qb):
        s = jnp.einsum('bqhd,bkhd->bhqk', qb, k, preferred_element_type=jnp.float32) * scale
        p = jax.nn.softmax(s, axis=-1)
        return jnp.einsum('bhqk,bkhd->bqhd', p.astype(v.dtype), v)

    out = lax.map(one_block, qp)
    out = jnp.moveaxis(out, 0, 1).reshape(b, nb * Q_BLOCK, H, V_HEAD_DIM)
    return out[:, :L]

def mla_mixer(u, w_in, q_norm, kv_norm, w_q_up, w_kv_up, q_head_norm, k_head_norm, w_out):
    b, L, _ = u.shape
    c_q, c_kv, k_rope = jnp.split(u @ w_in, [Q_LORA_RANK, Q_LORA_RANK + KV_LORA_RANK], axis=-1)
    q = (rmsnorm(c_q, q_norm) @ w_q_up).reshape(b, L, MLA_HEADS, QK_HEAD_DIM)
    kv = (rmsnorm(c_kv, kv_norm) @ w_kv_up).reshape(b, L, MLA_HEADS, QK_NOPE_DIM + V_HEAD_DIM)
    k_nope, v = jnp.split(kv, [QK_NOPE_DIM], axis=-1)
    k = jnp.concatenate(
        [k_nope, jnp.broadcast_to(k_rope[:, :, None, :], (b, L, MLA_HEADS, QK_ROPE_DIM))], axis=-1)
    q = rmsnorm(q, q_head_norm)
    k = rmsnorm(k, k_head_norm)
    pos = jnp.arange(L, dtype=jnp.float32)
    q = apply_rope(q, pos)
    k = apply_rope(k, pos)
    o = block_attention(q, k, v)
    return o.reshape(b, L, MLA_HEADS * V_HEAD_DIM) @ w_out

def depthwise_conv(x, w, bias):
    y = lax.conv_general_dilated(
        x, w[:, None, :].astype(x.dtype), window_strides=(1,),
        padding=[(D_CONV // 2, D_CONV // 2)],
        dimension_numbers=('NWC', 'WIO', 'NWC'), feature_group_count=x.shape[-1])
    return y + bias.astype(x.dtype)

def ssd_chunked(X, A, B, C):
    b, T = X.shape[0], X.shape[1]
    nc = T // CHUNK
    X = X.reshape(b, nc, CHUNK, SSD_GROUPS, HEADS_PER_GROUP, SSD_HEAD_DIM)
    A = A.reshape(b, nc, CHUNK, SSD_GROUPS, HEADS_PER_GROUP)
    B = B.reshape(b, nc, CHUNK, SSD_GROUPS, D_STATE)
    C = C.reshape(b, nc, CHUNK, SSD_GROUPS, D_STATE)
    a_cs = jnp.cumsum(A, axis=2)
    seg = a_cs[:, :, :, None] - a_cs[:, :, None, :]
    mask = jnp.tril(jnp.ones((CHUNK, CHUNK), dtype=bool))[:, :, None, None]
    l_mat = jnp.exp(jnp.where(mask, seg, -jnp.inf))
    y_diag = jnp.einsum('bclgn,bcsgn,bclsgj,bcsgjp->bclgjp', C, B, l_mat, X)
    decay_states = jnp.exp(a_cs[:, :, -1:] - a_cs)
    states = jnp.einsum('bclgn,bclgj,bclgjp->bcgjpn', B, decay_states, X)
    chunk_decay = jnp.exp(a_cs[:, :, -1])

    def step(carry, inp):
        st, dc = inp
        return carry * dc[..., None, None] + st, carry

    init = jnp.zeros((b, SSD_GROUPS, HEADS_PER_GROUP, SSD_HEAD_DIM, D_STATE), jnp.float32)
    _, prev = lax.scan(step, init, (jnp.moveaxis(states, 1, 0), jnp.moveaxis(chunk_decay, 1, 0)))
    prev = jnp.moveaxis(prev, 0, 1)
    y_off = jnp.einsum('bclgn,bcgjpn,bclgj->bclgjp', C, prev, jnp.exp(a_cs))
    return (y_diag + y_off).reshape(b, T, SSD_GROUPS, HEADS_PER_GROUP, SSD_HEAD_DIM)

def ssd_mixer(u, w_in, conv_w, conv_b, dt_bias, a_log, d_skip, norm_w, w_out):
    b, L, _ = u.shape
    z, xbc, dt_raw = jnp.split(u @ w_in, [D_INNER, D_INNER + CONV_DIM], axis=-1)
    xbc = jax.nn.silu(depthwise_conv(xbc, conv_w, conv_b))
    gn = SSD_GROUPS * D_STATE
    xs, bm, cm = jnp.split(xbc.astype(jnp.float32), [D_INNER, D_INNER + gn], axis=-1)
    xs = xs.reshape(b, L, SSD_GROUPS, HEADS_PER_GROUP, SSD_HEAD_DIM)
    bm = bm.reshape(b, L, SSD_GROUPS, D_STATE)
    cm = cm.reshape(b, L, SSD_GROUPS, D_STATE)
    dt = jax.nn.softplus(dt_raw.astype(jnp.float32).reshape(b, L, 2, SSD_GROUPS, HEADS_PER_GROUP)
                         + dt_bias.astype(jnp.float32).reshape(2, SSD_GROUPS, HEADS_PER_GROUP))
    a = -jnp.exp(a_log.astype(jnp.float32)).reshape(2, SSD_GROUPS, HEADS_PER_GROUP)

    def pad_front(t):
        return jnp.pad(t, ((0, 0), (META_PAD, 0)) + ((0, 0),) * (t.ndim - 2))

    xs_p, b_p, c_p, dt_p = pad_front(xs), pad_front(bm), pad_front(cm), pad_front(dt)

    def direction(d, reverse):
        fl = (lambda t: jnp.flip(t, axis=1)) if reverse else (lambda t: t)
        dt_d = fl(dt_p[:, :, d])
        y_d = ssd_chunked(fl(xs_p) * dt_d[..., None], dt_d * a[d], fl(b_p), fl(c_p))
        return fl(y_d)

    y = direction(0, False) + direction(1, True)
    y = y[:, META_PAD:] + d_skip.astype(jnp.float32).reshape(SSD_GROUPS, HEADS_PER_GROUP)[..., None] * xs
    y = y.reshape(b, L, D_INNER) * jax.nn.silu(z.astype(jnp.float32))
    y = rmsnorm(y, norm_w).astype(u.dtype)
    return y @ w_out

def swiglu(u, w_gate, w_up, w_down):
    return (jax.nn.silu(u @ w_gate) * (u @ w_up)) @ w_down

def encode(x, meta_tokens, mix_norm, ffn_norm, attn_p, ssd_p, ffn_p, final_norm):
    b = x.shape[0]
    meta = jnp.broadcast_to(meta_tokens.astype(x.dtype)[None], (b, N_META, D_MODEL))
    h = jnp.concatenate([meta, x], axis=1)
    ia, ib = 0, 0
    for layer in range(DEPTH):
        u = rmsnorm(h, mix_norm[layer])
        if layer % N_MIXERS == 0:
            h = h + mla_mixer(u, *[p[ia] for p in attn_p])
            ia += 1
        else:
            h = h + ssd_mixer(u, *[p[ib] for p in ssd_p])
            ib += 1
        u = rmsnorm(h, ffn_norm[layer])
        h = h + swiglu(u, *[p[layer] for p in ffn_p])
    h = rmsnorm(h, final_norm)
    return h[:, N_META:]

def setup_inputs(seed: int = 0) -> dict:
    key = jax.random.key(seed)
    ks = iter(jax.random.split(key, 40))

    def nrm(shape, scale):
        return jax.random.normal(next(ks), shape, jnp.float32) * scale

    def gain(shape):
        return 1.0 + nrm(shape, 0.02)

    out_scale = (2.0 * DEPTH) ** -0.5
    na, ns = N_ATTN_LAYERS, N_SSD_LAYERS
    dt0 = jnp.exp(jax.random.uniform(next(ks), (ns, 2, SSD_HEADS), jnp.float32,
                                     math.log(1e-3), math.log(1e-1)))
    dt_bias = dt0 + jnp.log(-jnp.expm1(-dt0))
    a_log = jnp.log(jax.random.uniform(next(ks), (ns, 2, SSD_HEADS), jnp.float32, 1.0, 16.0))
    return {
        'x_prompt': nrm((BATCH, SEQ, D_MODEL), 1.0),
        'x_sample': nrm((DEC_BATCH, DEC_SEQ, D_MODEL), 1.0),
        'meta_tokens': nrm((N_META, D_MODEL), 1.0),
        'mix_norm': gain((DEPTH, D_MODEL)),
        'ffn_norm': gain((DEPTH, D_MODEL)),
        'mla_w_in': nrm((na, D_MODEL, Q_LORA_RANK + KV_LORA_RANK + QK_ROPE_DIM), D_MODEL ** -0.5),
        'mla_q_norm': gain((na, Q_LORA_RANK)),
        'mla_kv_norm': gain((na, KV_LORA_RANK)),
        'mla_w_q_up': nrm((na, Q_LORA_RANK, MLA_HEADS * QK_HEAD_DIM), Q_LORA_RANK ** -0.5),
        'mla_w_kv_up': nrm((na, KV_LORA_RANK, MLA_HEADS * (QK_NOPE_DIM + V_HEAD_DIM)), KV_LORA_RANK ** -0.5),
        'mla_q_head_norm': gain((na, QK_HEAD_DIM)),
        'mla_k_head_norm': gain((na, QK_HEAD_DIM)),
        'mla_w_out': nrm((na, MLA_HEADS * V_HEAD_DIM, D_MODEL), (MLA_HEADS * V_HEAD_DIM) ** -0.5 * out_scale),
        'ssd_w_in': nrm((ns, D_MODEL, 2 * D_INNER + 2 * SSD_GROUPS * D_STATE + 2 * SSD_HEADS), D_MODEL ** -0.5),
        'ssd_conv_w': nrm((ns, D_CONV, CONV_DIM), D_CONV ** -0.5),
        'ssd_conv_b': nrm((ns, CONV_DIM), 0.01),
        'ssd_dt_bias': dt_bias,
        'ssd_a_log': a_log,
        'ssd_d': gain((ns, SSD_HEADS)),
        'ssd_norm': gain((ns, D_INNER)),
        'ssd_w_out': nrm((ns, D_INNER, D_MODEL), D_INNER ** -0.5 * out_scale),
        'ffn_w_gate': nrm((DEPTH, D_MODEL, FFN_HIDDEN), D_MODEL ** -0.5),
        'ffn_w_up': nrm((DEPTH, D_MODEL, FFN_HIDDEN), D_MODEL ** -0.5),
        'ffn_w_down': nrm((DEPTH, FFN_HIDDEN, D_MODEL), FFN_HIDDEN ** -0.5 * out_scale),
        'final_norm': gain((D_MODEL,)),
    }

def reference(x_prompt, x_sample, meta_tokens, mix_norm, ffn_norm,
              mla_w_in, mla_q_norm, mla_kv_norm, mla_w_q_up, mla_w_kv_up,
              mla_q_head_norm, mla_k_head_norm, mla_w_out,
              ssd_w_in, ssd_conv_w, ssd_conv_b, ssd_dt_bias, ssd_a_log, ssd_d, ssd_norm, ssd_w_out,
              ffn_w_gate, ffn_w_up, ffn_w_down, final_norm):
    attn_p = (mla_w_in, mla_q_norm, mla_kv_norm, mla_w_q_up, mla_w_kv_up,
              mla_q_head_norm, mla_k_head_norm, mla_w_out)
    ssd_p = (ssd_w_in, ssd_conv_w, ssd_conv_b, ssd_dt_bias, ssd_a_log, ssd_d, ssd_norm, ssd_w_out)
    ffn_p = (ffn_w_gate, ffn_w_up, ffn_w_down)
    y_prompt = encode(x_prompt, meta_tokens, mix_norm, ffn_norm, attn_p, ssd_p, ffn_p, final_norm)
    y_sample = encode(x_sample, meta_tokens, mix_norm, ffn_norm, attn_p, ssd_p, ffn_p, final_norm)
    return (y_prompt, y_sample)


_drawn_inputs = setup_inputs


def setup_inputs(seed=0):
    import zlib

    import numpy as np

    out = dict(_drawn_inputs(seed))
    spreads = {}
    factors = {'mix_norm': 4.183,
     'ffn_norm': 4.657,
     'mla_q_norm': 8.0,
     'mla_kv_norm': 8.0,
     'mla_q_head_norm': 8.0,
     'mla_k_head_norm': 8.0,
     'ssd_conv_b': 49.212,
     'ssd_d': 64.0,
     'ssd_norm': 44.849,
     'final_norm': 8.132}
    for name, (base, spread) in spreads.items():
        noise = np.random.default_rng([zlib.crc32(name.encode()), seed]).standard_normal(out[name].shape)
        drawn = base * np.exp(spread * noise) if base else spread * noise
        out[name] = __import__('jax').numpy.asarray(drawn.astype(out[name].dtype))
    for name, factor in factors.items():
        out[name] = (out[name] * factor).astype(out[name].dtype)
    return out
```

```python
import math
from contextlib import ExitStack, contextmanager

import numpy as np

import concourse.bass as bass
from concourse import mybir

F32 = mybir.dt.float32
F32R = mybir.dt.float32r
I32 = mybir.dt.int32
ALU = mybir.AluOpType
ACT = mybir.ActivationFunctionType
AX_X = mybir.AxisListType.X
AX_XY = mybir.AxisListType.XY

P = 128
D_MODEL = 1024
N_META = 16
SEQ = 512
NSEQ = 2
L = N_META + SEQ
T = NSEQ * L
CH = 88
NC = T // CH
CS = L // CH
NB = 3
NT = T // NB
CB = NC // NB
KD = D_MODEL // P
EPS = 1e-6

HEADS, NOPE, ROPE, VD = 16, 64, 32, 64
QK = NOPE + ROPE
PAIRS = HEADS // 2
Q_RANK, KV_RANK = 384, 256
KQ, KKV = Q_RANK // P, KV_RANK // P

D_INNER, GROUPS, D_STATE, D_CONV, SHEADS, SP_ = 2048, 4, 128, 5, 32, 64
CONV_TILES = (D_INNER + 2 * GROUPS * D_STATE) // P
Z_TILES = D_INNER // P
TILES_PER_GROUP = Z_TILES // GROUPS
HPG = SHEADS // GROUPS

FFN = 2816
F_TILES = FFN // P
F_STEP = 2
F_STEPS = F_TILES // F_STEP

BLK = 8

U_MLA_IN = KQ + KKV + 1
U_PAIR = 2
U_OUT = KD
U_FFN = F_TILES * 3
U_DT = 1
U_SSD_IN = CONV_TILES + Z_TILES
U_SSD_OUT = Z_TILES * KD // BLK
U0_PAIR = U_MLA_IN
U0_OUT = U0_PAIR + PAIRS * U_PAIR
U0_FFN0 = U0_OUT + U_OUT
U0_DT = U0_FFN0 + U_FFN
U0_SSD_IN = U0_DT + U_DT
U0_SSD_OUT = U0_SSD_IN + U_SSD_IN
U0_FFN1 = U0_SSD_OUT + U_SSD_OUT
UNITS = U0_FFN1 + U_FFN

COLS = {}
_n = 0
for _name, _w in (("mix0", KD), ("ffn0", KD), ("mix1", KD), ("ffn1", KD), ("final", KD),
                  ("q_norm", KQ), ("kv_norm", KKV), ("q_head", 2), ("k_nope", 1), ("k_rope", 1),
                  ("conv", CONV_TILES * (D_CONV + 1)), ("skip", Z_TILES), ("ssd_norm", Z_TILES)):
    COLS[_name] = _n
    _n += _w
NCOLS = _n

C_IDENT, C_PAIR, C_UPPER, C_LOWER, C_ONES, C_STRICT_LOWER, C_STRICT_UPPER, C_MASK = (P * k for k in range(8))

B_SCAN, B_FFN1, B_LAST = 1, 1, 1
M_QE, M_QO, M_KE, M_KO, M_ROPE = range(5)
NCONST = C_MASK + 5

S_R1, S_R1SQ, S_A, S_B, S_A2, S_B2, S_RR, S_V, S_TMP, S_QS, S_KF = 0, 1, 2, 3, 4, 5, 6, 7, 9, 11, 13

INPUTS = ("x", "w", "cols", "rows", "const", "trig")


class Counts:

    def __init__(self):
        self.seen, self.made, self.running = {}, {}, []

    def _value(self, which, sem):
        n = (self.seen, self.made)[which].get(sem.name, 0)
        for i, per in self.running:
            if per[which].get(sem.name, 0):
                n = i * per[which][sem.name] + n
        return n

    def want(self, sem, k=1):
        self.seen[sem.name] = self.seen.get(sem.name, 0) + k
        return self._value(0, sem)

    def ahead(self, sem, k=1):
        return self._value(0, sem) + k

    def adds(self, sem, k=1):
        self.made[sem.name] = self.made.get(sem.name, 0) + k
        return k

    def given(self, sem):
        assert self.made.get(sem.name, 0) > 0
        return self._value(1, sem)

    @contextmanager
    def rounds(self, trips, i, seen, made):
        per = ({s.name: k for s, k in seen.items()}, {s.name: k for s, k in made.items()})
        start = (dict(self.seen), dict(self.made))
        self.running.append((i, per))
        yield
        self.running.pop()
        for which, counts in enumerate((self.seen, self.made)):
            found = {s: n - start[which].get(s, 0) for s, n in counts.items() if n != start[which].get(s, 0)}
            if found != {s: k for s, k in per[which].items() if k}:
                raise ValueError(f"{('seen', 'made')[which]} per round: {found}")
            for s, k in found.items():
                counts[s] = start[which].get(s, 0) + trips * k


def chunks(ap):
    return ap.rearrange("p (c t) -> p c t", t=CH)


def banks(ap):
    return ap.rearrange("p (b n) -> p b n", b=NB)


def seqs(ap):
    return ap.rearrange("p (s n) -> p s n", s=NSEQ)


def encoder(nc, tensors):
    base = ExitStack()

    def sem(name):
        return base.enter_context(nc.semaphore(name))

    def sb(name, shape, dt=F32, stack=None):
        return (stack or base).enter_context(nc.sbuf_tensor(name, shape, dt))

    x_d, w_d, cols_d, rows_d, const_d, trig_d, out_d = (tensors[n] for n in INPUTS + ("out",))
    xbc_d = nc.dram_tensor("xbc_scratch", (CONV_TILES, P, T), F32, kind="Internal").ap()
    z_d = nc.dram_tensor("z_scratch", (Z_TILES, P, T), F32, kind="Internal").ap()
    h_d = nc.dram_tensor("h_scratch", (KD, P, T), F32, kind="Internal").ap()

    Wraw = [sb(f"Wraw{s}", [P, BLK, P]) for s in range(2)]
    Whi = [sb(f"Whi{s}", [P, BLK, P], F32R) for s in range(2)]
    Wlo = [sb(f"Wlo{s}", [P, BLK, P], F32R) for s in range(2)]
    H = sb("H", [P, KD, T])
    cols = sb("cols", [P, NCOLS])
    const = sb("const", [P, NCONST])
    STAT = sb("STAT", [CH, 26, NC])
    SQ = sb("SQ", [P, T])
    SS = sb("SS", [P, T])
    RMS = sb("RMS", [P, T])

    KS = sb("KS", [CH, NC, 4])
    SMAX, SSUM, SINV = (sb(n, [CH, 2 * NC]) for n in ("SMAX", "SSUM", "SINV"))

    ident = const[:, C_IDENT:C_IDENT + P]
    ident_ch = const[0:CH, C_IDENT:C_IDENT + CH]
    pair_sum = const[:, C_PAIR:C_PAIR + P]
    upper = const[0:CH, C_UPPER:C_UPPER + CH]
    lower = const[0:CH, C_LOWER:C_LOWER + CH]
    strict_lower = const[0:CH, C_STRICT_LOWER:C_STRICT_LOWER + CH]
    strict_upper = const[0:CH, C_STRICT_UPPER:C_STRICT_UPPER + CH]
    one = const[:, C_ONES:C_ONES + 1]
    ones = const[:, C_ONES:C_ONES + P]
    ones_ch = const[0:CH, C_ONES:C_ONES + P]

    def mask(k, n=1):
        return const[:, C_MASK + k:C_MASK + k + n]

    def col(name, k=0, n=1):
        return cols[:, COLS[name] + k:COLS[name] + k + n]

    def stat(k, n=1):
        return STAT[:, k, :] if n == 1 else STAT[:, k:k + n, :]

    low = ExitStack()
    Uhi, Ulo = sb("Uhi", [P, KD, T], F32R, low), sb("Ulo", [P, KD, T], F32R, low)
    with ExitStack() as s:
        Chi, Clo = sb("Chi", [P, KQ + KKV, T], F32R, s), sb("Clo", [P, KQ + KKV, T], F32R, s)
        KR = [sb(f"KR{h}", [P, T], F32, s) for h in range(2)]
        SSQ = [sb(f"SSQ{k}", [P, T], F32, s) for k in range(2)]
        CF = [sb(f"CF{k}", [P, T], F32, s) for k in range(2)]
    trig_k = RMS[:, 0:L]
    with ExitStack() as s:
        Ohi, Olo = sb("Ohi", [P, KD, T], F32R, s), sb("Olo", [P, KD, T], F32R, s)
    with ExitStack() as s:
        GATE, SILU, HID = (sb(n, [P, T], F32, s) for n in ("GATE", "SILU", "HID"))
        HIDhi, HIDlo = sb("HIDhi", [P, F_STEP, T], F32R, s), sb("HIDlo", [P, F_STEP, T], F32R, s)
    with ExitStack() as s:
        DT, A, CSUM, WST = (sb(n, [CH, 2, NC, SHEADS], F32, s) for n in ("DT", "A", "CSUM", "WST"))
        DECAY = sb("DECAY", [P, 2, NC, SHEADS], F32, s)
        with ExitStack() as s2:
            XC = sb("XC", [P, T], F32, s2)
            YC = [sb(f"YC{k}", [P, T], F32, s2) for k in range(2)]
            E1, E2, E3 = (sb(n, [CH, 2, NC, SHEADS], F32, s2) for n in ("E1", "E2", "E3"))
            ROWS = sb("ROWS", [CH, 2, 2, SHEADS], F32, s2)
            TAPS = sb("TAPS", [P, D_CONV + 1], F32, s2)
        with ExitStack() as s2:
            M = [sb(f"M{h}", [P, T], F32, s2) for h in range(2)]
            XW = [sb(f"XW{d}", [CH, NC, P], F32, s2) for d in range(2)]
            ST = [sb(f"ST{d}", [P, NC, P], F32, s2) for d in range(2)]
            CARRY = sb("CARRY", [P, NSEQ, 2, SP_], F32, s2)
            Yhi, Ylo = sb("Yhi", [P, 2, T], F32R, s2), sb("Ylo", [P, 2, T], F32R, s2)
    low.close()
    with ExitStack() as s:
        Q = [sb(f"Q{h}", [P, T], F32, s) for h in range(2)]
        QR = [sb(f"QR{h}", [P, T], F32, s) for h in range(2)]
        SQH = [sb(f"SQH{h}", [P, T], F32, s) for h in range(3)]
        KM = [sb(f"KM{h}", [P, T], F32, s) for h in range(2)]
        V = sb("V", [CH, NC, P], F32, s)
        PR = [sb(f"PR{h}", [CH, L], F32, s) for h in range(2)]
        PT = [sb(f"PT{h}", [CH, CS, CH], F32, s) for h in range(2)]
        O = sb("O", [CH, NC, P], F32, s)
        trig_q = sb("trig_q", [P, 2, L], F32, s)
    with ExitStack() as s:
        BT, CT, XT, ZT, Y = (sb(n, [P, T], F32, s) for n in ("BT", "CT", "XT", "ZT", "Y"))
        BTOK, XTOK = sb("BTOK", [CH, NC, P], F32, s), sb("XTOK", [CH, NC, P], F32, s)
        G = [sb(f"G{d}", [CH, NC, CH], F32, s) for d in range(2)]
        W = [sb(f"W{d}", [CH, NC, CH], F32, s) for d in range(2)]
        TM, T2 = sb("TM", [CH, NC, CH], F32, s), sb("T2", [P, T], F32, s)
        EB = [sb("EB", [P, T], F32, s), RMS]
        AG, DTG, WG = (sb(n, [CH, 2, NC, HPG], F32, s) for n in ("AG", "DTG", "WG"))
        DECG = sb("DECG", [P, 2, NC, HPG], F32, s)
        SKIPG, NORMG = (sb(n, [P, TILES_PER_GROUP], F32, s) for n in ("SKIPG", "NORMG"))

    PS = base.enter_context(nc.psum_tensor("PS", [P, 8, 512], F32))
    STAT_BANK = 6

    def group(b, n=NT, parts=P, at=0):
        return PS[at:at + parts, NB * b:NB * b + NB, 0:n]

    def piece(b, c, width, parts=CH, at=0):
        k = c % CB * width
        return PS[at:at + parts, NB * b + c // CB, k:k + width]

    raw_full = [sem(f"raw_full{s}") for s in range(2)]
    w_full = [sem(f"w_full{s}") for s in range(2)]
    w_free = [sem(f"w_free{s}") for s in range(2)]
    to_vector = [sem(f"to_vector{b}") for b in range(2)]
    to_scalar = [sem(f"to_scalar{b}") for b in range(2)]
    grp_free = [sem(f"grp_free{b}") for b in range(2)]
    vec_steps, act_steps, pool_steps = sem("vec_steps"), sem("act_steps"), sem("pool_steps")
    const_in = sem("const_in")
    x_in = [sem(f"x_in{k}") for k in range(KD)]
    h_ready = sem("h_ready")
    hi_ready, u_ready = sem("hi_ready"), sem("u_ready")
    sq_full, sq_free, sum_ready = sem("sq_full"), sem("sq_free"), sem("sum_ready")
    stat_full, row_ready = sem("stat_full"), sem("row_ready")
    scan_free = sem("scan_free")
    rms_ready = sem("rms_ready")
    trig_in, rope_sq, rope_ready = sem("trig_in"), sem("rope_sq"), sem("rope_ready")
    q_squared, k_squared = sem("q_squared"), sem("k_squared")
    q_ready, ks_ready = sem("q_ready"), sem("ks_ready")
    km_ready, v_ready = sem("km_ready"), sem("v_ready")
    sc_full, nb_ready, p_full = sem("sc_full"), sem("nb_ready"), sem("p_full")
    pt_full, pt_ready, rinv_ready = sem("pt_full"), sem("pt_ready"), sem("rinv_ready")
    ov_full, ov_free, o_ready = sem("ov_full"), sem("ov_free"), sem("o_ready")
    o_split, h_loaded = sem("o_split"), sem("h_loaded")
    gate_ready, silu_ready, hid_ready = sem("gate_ready"), sem("silu_ready"), sem("hid_ready")
    hid_hi, hid_split = sem("hid_hi"), sem("hid_split")
    out_ready, out_done = sem("out_ready"), sem("out_done")
    yc_ready, yc_out = sem("yc_ready"), [sem(f"yc_out{k}") for k in range(2)]
    rows_in, h_saved = sem("rows_in"), sem("h_saved")
    exp_in, exp_out, a_ready = sem("exp_in"), sem("exp_out"), sem("a_ready")
    staged, w_built, w_read = sem("staged"), sem("w_built"), sem("w_read")
    bt_in, ct_in, xt_in, zt_in = sem("bt_in"), sem("ct_in"), sem("xt_in"), sem("zt_in")
    btok_ready, g_ready = sem("btok_ready"), sem("g_ready")
    xtok_ready, y0_ready, l_ready, m_ready = (sem(n) for n in ("xtok_ready", "y0_ready", "l_ready", "m_ready"))
    eb_ready, xw_ready, st_ready = sem("eb_ready"), sem("xw_ready"), sem("st_ready")
    y_ready, y_hi, y_split, h_back = sem("y_ready"), sem("y_hi"), sem("y_split"), [sem(f"h_back{k}") for k in range(2)]

    block = base.enter_context(nc.Block())

    def dcol(tensor, d, h):
        return tensor[:, d, :, h]

    @block.sync
    def _(sp):
        c = Counts()

        def load(u, s):
            sp.dma_start(Wraw[s][:], w_d[u].rearrange("p (k m) -> p k m", m=P)
                         if isinstance(u, int) else
                         w_d[bass.ds(u, 1)].rearrange("o p (k m) -> p (o k) m", m=P)).then_inc(raw_full[s], 16)

        for u in range(2):
            load(u, u)
        pairs = (UNITS - 2) // 2
        with sp.Fori(0, pairs) as i, \
                c.rounds(pairs, i,
                         {w_full[0]: 1, w_full[1]: 1},
                         {}):
            for s in range(2):
                sp.wait_ge(w_full[s], c.want(w_full[s]))
                load(i * 2 + (2 + s), s)
        for u in range(2 + 2 * pairs, UNITS):
            sp.wait_ge(w_full[u % 2], c.want(w_full[u % 2]))
            load(u, u % 2)

    @block.gpsimd
    def _(pool):
        c = Counts()

        def split(s):
            pool.wait_ge(raw_full[s], c.want(raw_full[s], 16))
            pool.wait_ge(w_free[s], c.want(w_free[s]))
            pool.tensor_tensor(Whi[s][:], Wraw[s][:], ones.unsqueeze(1).broadcast_to([P, BLK, P]), ALU.mult)\
                .then_inc(pool_steps, c.adds(pool_steps))
            pool.wait_ge(pool_steps, c.given(pool_steps))
            pool.tensor_tensor(Wlo[s][:], Wraw[s][:], Whi[s][:].bitcast(F32), ALU.subtract)\
                .then_inc(w_full[s], c.adds(w_full[s]))

        def split_units(u0, n):
            per = {pool_steps: 2, w_full[0]: 1, w_full[1]: 1}
            with pool.Fori(0, n // 2) as i, \
                    c.rounds(n // 2, i,
                             {raw_full[0]: 16, raw_full[1]: 16, w_free[0]: 1, w_free[1]: 1},
                             per):
                for k in range(2):
                    split((u0 + k) % 2)
            if n % 2:
                split((u0 + n - 1) % 2)

        pool.wait_ge(const_in, c.want(const_in, 16 * 2))
        split_units(0, U0_SSD_OUT)

        def build_w(h):
            pool.wait_ge(w_read, c.want(w_read))
            for d, m in ((0, strict_lower), (1, strict_upper)):
                ins = pool.tensor_tensor(W[d][:], m.unsqueeze(1).broadcast_to([CH, NC, CH]),
                                         dcol(AG, d, h).unsqueeze(2).broadcast_to([CH, NC, CH]), ALU.mult)
                ins.then_inc(pool_steps, c.adds(pool_steps))
            pool.wait_ge(pool_steps, c.given(pool_steps))
            pool.sem_inc(w_built, 1)

        with pool.Fori(0, GROUPS) as i, \
                c.rounds(GROUPS, i,
                         {staged: 1, w_read: HPG, **{raw_full[k]: 32 for k in range(2)},
                          **{w_free[k]: 2 for k in range(2)}},
                         {pool_steps: 2 * HPG + 4, w_full[0]: 2, w_full[1]: 2}):
            pool.wait_ge(staged, c.want(staged))
            for j in range(TILES_PER_GROUP):
                build_w(2 * j)
                build_w(2 * j + 1)
                for u in ((0,), (), (1, 2), (3,))[j]:
                    split((U0_SSD_OUT + u) % 2)
        split_units(U0_FFN1, U_FFN)

    @block.tensor
    def _(pe):
        c = Counts()
        now = {"slot": None, "release": None}

        def mm(out, lhsT, rhs, start=True, stop=True):
            ins = pe.matmul(out, lhsT, rhs, start=start, stop=stop, skip_group_check=True)
            if now["release"] is not None:
                ins.then_inc(w_free[now["release"]], c.adds(w_free[now["release"]]))
                now["release"] = None
            return ins

        def enter_unit(u):
            s = u % 2
            pe.wait_ge(w_full[s], c.want(w_full[s]))
            now["release"], now["slot"] = now["slot"], s

        def product(out, blocks, Xhi, Xlo, kts, ready=None, n0=0, k_total=None):
            last = (k_total or len(kts)) - 1
            for j, (blk, kt) in enumerate(zip(blocks, kts)):
                if ready is not None:
                    pe.wait_ge(ready, c.want(ready))
                for p, (W, X) in enumerate(((Whi, Xhi), (Whi, Xlo), (Wlo, Xhi))):
                    for n in range(NB):
                        ins = mm(out[:, n, :], W[now["slot"]][:, blk, :], X[:, kt, n * NT:(n + 1) * NT],
                                 start=(j == 0 and p == 0), stop=(j == last and p == 2))
            return ins

        def sums_by_token(k, src, rhs):
            n = rhs.shape[1]
            for ch in range(NC):
                ins = mm(PS[0:CH, STAT_BANK, k * NC:(k + n) * NC].rearrange("p (k c) -> p k c", c=NC)[:, :, ch],
                         src[:, ch * CH:(ch + 1) * CH], rhs)
            return ins

        def spread_rms(b):
            pe.wait_ge(row_ready, c.want(row_ready))
            pe.wait_ge(grp_free[b], c.want(grp_free[b]))
            for ch in range(NC):
                ins = mm(piece(b, ch, CH, P), STAT[:, S_R1, ch:ch + 1].broadcast_to([CH, P]), ident_ch)
            ins.then_inc(to_scalar[b], c.adds(to_scalar[b]))

        pe.wait_ge(const_in, c.want(const_in, 16 * 2))
        for m in range(U_MLA_IN):
            enter_unit(m)
            pe.wait_ge(grp_free[m % 2], c.want(grp_free[m % 2]))
            product(group(m % 2), range(KD), Uhi, Ulo, range(KD), u_ready if m == 0 else None)\
                .then_inc(to_scalar[m % 2], c.adds(to_scalar[m % 2]))
        pe.wait_ge(sum_ready, c.want(sum_ready))
        sums_by_token(0, SS, one)
        pe.wait_ge(sum_ready, c.want(sum_ready))
        sums_by_token(1, SSQ[0], one)
        pe.wait_ge(sum_ready, c.want(sum_ready))
        sums_by_token(2, SSQ[1], one)
        pe.wait_ge(rope_sq, c.want(rope_sq))
        sums_by_token(3, SQ, mask(M_ROPE)).then_inc(stat_full, c.adds(stat_full))
        pe.wait_ge(rope_ready, c.want(rope_ready))
        pe.wait_ge(grp_free[0], c.want(grp_free[0]))
        for n in range(NB):
            ins = mm(group(0)[:, n, :], pair_sum, CF[0][:, n * NT:(n + 1) * NT])
        ins.then_inc(to_scalar[0], c.adds(to_scalar[0]))
        pe.wait_ge(u_ready, c.want(u_ready, KQ + KKV))
        pe.wait_ge(row_ready, c.want(row_ready))

        steps = [(h, s, t) for h in range(2) for s in range(NSEQ) for t in range(CS)]
        NS = len(steps)

        def attention_round():
            enter_unit(U0_PAIR)
            for h in range(3):
                b = h % 2
                pe.wait_ge(grp_free[b], c.want(grp_free[b]))
                if h < 2:
                    ins = product(group(b), range(KQ * h, KQ * h + KQ), Chi, Clo, range(KQ))
                else:
                    ins = product(group(b), range(2 * KQ, 2 * KQ + KKV), Chi, Clo, range(KQ, KQ + KKV))
                ins.then_inc(to_scalar[b], c.adds(to_scalar[b]))
            enter_unit(U0_PAIR + 1)
            pe.wait_ge(grp_free[1], c.want(grp_free[1]))
            for ch in range(NC):
                t = slice(ch * CH, (ch + 1) * CH)
                for k in range(KKV):
                    for p, (X, W) in enumerate(((Chi, Whi), (Clo, Whi), (Chi, Wlo))):
                        ins = mm(piece(1, ch, P), X[:, KQ + k, t], W[now["slot"]][:, k, :],
                                 start=(k == 0 and p == 0), stop=(k == KKV - 1 and p == 2))
            ins.then_inc(to_vector[1], c.adds(to_vector[1]))
            for h in range(3):
                pe.wait_ge(q_squared if h < 2 else k_squared, c.want(q_squared if h < 2 else k_squared))
                ins = sums_by_token(h, SQH[h], mask((M_QE, M_QO, M_KE)[h], 1 + (h == 2)))
            ins.then_inc(stat_full, c.adds(stat_full))
            pe.wait_ge(ks_ready, c.want(ks_ready))
            for h in range(2):
                pe.wait_ge(grp_free[h], c.want(grp_free[h]))
                for ch in range(NC):
                    for part in range(2):
                        ins = mm(piece(h, ch, CH, NOPE, part * NOPE),
                                 KS[:, ch, 2 * h + part:2 * h + part + 1].broadcast_to([CH, NOPE]), ident_ch)
                ins.then_inc(to_vector[h], c.adds(to_vector[h]))
            pe.wait_ge(q_ready, c.want(q_ready, 2))
            pe.wait_ge(v_ready, c.want(v_ready))
            pe.wait_ge(grp_free[0], c.ahead(grp_free[0]))
            pe.wait_ge(grp_free[1], c.ahead(grp_free[1]))
            pe.wait_ge(km_ready, c.want(km_ready, 2))
            for n in range(NS + 2):
                if n < NS:
                    h, s, t = steps[n]
                    at = (s * CS + t) * CH
                    for j in range(2):
                        ins = mm(PS[0:CH, 2 * (n % 2) + j, 0:L // 2], Q[h][:, at:at + CH],
                                 KM[h][:, s * L + j * (L // 2):s * L + (j + 1) * (L // 2)])
                    ins.then_inc(sc_full, c.adds(sc_full))
                if n >= 2:
                    pe.wait_ge(pt_ready, c.want(pt_ready))
                if 1 <= n <= NS:
                    pe.wait_ge(p_full, c.want(p_full))
                    for j in range(CS):
                        ins = pe.transpose(PS[0:CH, 4 + j // 3, j % 3 * CH:(j % 3 + 1) * CH],
                                           PR[(n - 1) % 2][:, j * CH:(j + 1) * CH], ident_ch)
                    ins.then_inc(pt_full, c.adds(pt_full))
                if n >= 2:
                    h, s, t = steps[n - 2]
                    pe.wait_ge(ov_free, c.want(ov_free))
                    for j in range(CS):
                        ins = mm(PS[0:CH, 6 + n % 2, 0:VD], PT[n % 2][:, j, :],
                                 V[:, s * CS + j, h * VD:(h + 1) * VD], start=(j == 0), stop=(j == CS - 1))
                    ins.then_inc(ov_full, c.adds(ov_full))
            pe.wait_ge(ov_free, c.ahead(ov_free, 2))
            pe.wait_ge(grp_free[0], c.want(grp_free[0]))
            for ch in range(NC):
                ins = pe.transpose(piece(0, ch, CH, P), O[:, ch, :], ident_ch)
            ins.then_inc(to_scalar[0], c.adds(to_scalar[0]))

        with pe.Fori(0, PAIRS) as i, \
                c.rounds(PAIRS, i,
                         {w_full[0]: 1, w_full[1]: 1, grp_free[0]: 4, grp_free[1]: 3, q_squared: 2,
                          k_squared: 1, ks_ready: 1, q_ready: 2, v_ready: 1, km_ready: 2, pt_ready: NS,
                          p_full: NS, ov_free: NS},
                         {w_free[0]: 1, w_free[1]: 1, to_scalar[0]: 3, to_scalar[1]: 1, to_vector[0]: 1,
                          to_vector[1]: 2, stat_full: 1, sc_full: NS, pt_full: NS, ov_full: NS}):
            attention_round()

        for m in range(U_OUT):
            enter_unit(U0_OUT + m)
            pe.wait_ge(grp_free[m % 2], c.want(grp_free[m % 2]))
            product(group(m % 2), range(KD), Ohi, Olo, range(KD), o_split if m == 0 else None)\
                .then_inc(to_vector[m % 2], c.adds(to_vector[m % 2]))

        def feed_forward(u0, b0):
            b = [b0]

            def grp():
                b[0] ^= 1
                return b[0] ^ 1

            def column(u, ready=None):
                g = grp()
                enter_unit(u)
                pe.wait_ge(grp_free[g], c.want(grp_free[g]))
                product(group(g), range(KD), Uhi, Ulo, range(KD), ready).then_inc(to_vector[g], c.adds(to_vector[g]))

            def down(u):
                pe.wait_ge(hid_split, c.want(hid_split, F_STEP))
                for m in range(KD):
                    if m % (BLK // F_STEP) == 0:
                        enter_unit(u + m // (BLK // F_STEP))
                    g = grp()
                    pe.wait_ge(grp_free[g], c.want(grp_free[g]))
                    product(group(g), [m * F_STEP % BLK + k for k in range(F_STEP)],
                            HIDhi, HIDlo, range(F_STEP)).then_inc(to_vector[g], c.adds(to_vector[g]))

            column(u0, u_ready)
            pe.wait_ge(sum_ready, c.want(sum_ready))
            sums_by_token(0, SS, one).then_inc(stat_full, c.adds(stat_full))
            spread_rms(grp())
            for k in range(1, 2 * F_STEP):
                column(u0 + k)
            per = 2 * F_STEP + 2
            with pe.Fori(0, F_STEPS - 1) as i, \
                    c.rounds(F_STEPS - 1, i,
                             {w_full[0]: 3, w_full[1]: 3, grp_free[0]: 6, grp_free[1]: 6, hid_split: F_STEP},
                             {w_free[0]: 3, w_free[1]: 3, to_vector[0]: 6, to_vector[1]: 6}):
                column(u0 + 2 * F_STEP)
                down(u0 + 2 * F_STEP + 1)
                for k in range(1, 2 * F_STEP):
                    column(u0 + 2 * F_STEP + 2 + k)
            down(u0 + 2 * F_STEP + per * (F_STEPS - 1))
            return b[0]

        b = feed_forward(U0_FFN0, 0)

        def other(b):
            return b ^ 1

        enter_unit(U0_DT)
        pe.wait_ge(u_ready, c.want(u_ready, KD))
        pe.wait_ge(grp_free[b], c.want(grp_free[b]))
        for ch in range(NC):
            t = slice(ch * CH, (ch + 1) * CH)
            for k in range(KD):
                for p, (X, Wt) in enumerate(((Uhi, Whi), (Ulo, Whi), (Uhi, Wlo))):
                    ins = mm(piece(b, ch, 2 * SHEADS), X[:, k, t], Wt[now["slot"]][:, k, 0:2 * SHEADS],
                             start=(k == 0 and p == 0), stop=(k == KD - 1 and p == 2))
        ins.then_inc(to_vector[b], c.adds(to_vector[b]))
        pe.wait_ge(sum_ready, c.want(sum_ready))
        sums_by_token(0, SS, one).then_inc(stat_full, c.adds(stat_full))
        spread_rms(other(b))
        for u0, n in ((U0_SSD_IN, CONV_TILES), (U0_SSD_IN + CONV_TILES, Z_TILES)):
            with pe.Fori(0, n // 2) as i, \
                    c.rounds(n // 2, i,
                             {w_full[0]: 1, w_full[1]: 1, grp_free[0]: 1, grp_free[1]: 1},
                             {w_free[0]: 1, w_free[1]: 1, to_vector[0]: 1, to_vector[1]: 1}):
                for k, g in ((0, b), (1, other(b))):
                    enter_unit(u0 + k)
                    pe.wait_ge(grp_free[g], c.want(grp_free[g]))
                    product(group(g), range(KD), Uhi, Ulo, range(KD)).then_inc(to_vector[g], c.adds(to_vector[g]))
        pe.wait_ge(a_ready, c.want(a_ready))
        for g, by in ((b, (upper, lower)), (other(b), (ones_ch, ones_ch))):
            pe.wait_ge(grp_free[g], c.want(grp_free[g]))
            for d in range(2):
                ins = mm(PS[0:by[d].shape[1], NB * g + d, 0:NC * SHEADS], by[d],
                         A[:, d].rearrange("p c h -> p (c h)"))
            ins.then_inc(to_vector[g], c.adds(to_vector[g]))

        def scan_round():
            gb = [b]

            def grp():
                gb[0] ^= 1
                pe.wait_ge(grp_free[gb[0] ^ 1], c.want(grp_free[gb[0] ^ 1]))
                return gb[0] ^ 1

            def chunk(ap, ch):
                return ap[:, ch * CH:(ch + 1) * CH]

            def transposes(src):
                g = grp()
                for ch in range(NC):
                    ins = pe.transpose(piece(g, ch, P), chunk(src, ch), ident)
                ins.then_inc(to_scalar[g], c.adds(to_scalar[g]))

            def decays(h):
                pe.wait_ge(w_built, c.want(w_built))
                g = grp()
                for ch in range(NC):
                    mm(piece(g, ch, CH), W[0][:, ch, :], upper, stop=False)
                    ins = mm(piece(g, ch, CH), W[1][:, ch, :], lower, start=False)
                ins.then_inc(to_scalar[g], c.adds(to_scalar[g]))

            def running_sums(d, h):
                g = grp()
                for ch in range(NC):
                    for e in range(2):
                        ins = mm(piece(g, ch, CH, SP_, e * SP_),
                                 AG[:, d, ch, h + e:h + e + 1].broadcast_to([CH, SP_]), (upper, lower)[d])
                ins.then_inc(to_scalar[g], c.adds(to_scalar[g]))

            def out_projection(u):
                pe.wait_ge(y_split, c.want(y_split, 2))
                for m in range(KD):
                    if m % (BLK // 2) == 0:
                        enter_unit(u + m // (BLK // 2))
                    g = grp()
                    product(group(g), [m * 2 % BLK + k for k in range(2)], Yhi, Ylo, range(2))\
                        .then_inc(to_vector[g], c.adds(to_vector[g]))

            pe.wait_ge(staged, c.want(staged))
            pe.wait_ge(bt_in, c.want(bt_in, 16))
            transposes(BT)
            pe.wait_ge(ct_in, c.want(ct_in, 16))
            g = grp()
            for ch in range(NC):
                ins = mm(piece(g, ch, CH), chunk(BT, ch), chunk(CT, ch))
            ins.then_inc(to_vector[g], c.adds(to_vector[g]))
            for j in range(TILES_PER_GROUP):
                h = 2 * j
                pe.wait_ge(xt_in, c.want(xt_in, 16))
                transposes(XT)
                decays(h)
                running_sums(0, h)
                running_sums(1, h)
                decays(h + 1)
                if j == 0:
                    pe.wait_ge(btok_ready, c.want(btok_ready))
                for d in range(2):
                    pe.wait_ge(xw_ready, c.want(xw_ready))
                    g = grp()
                    for ch in range(NC):
                        ins = mm(piece(g, ch, P, P), BTOK[:, ch, :], XW[d][:, ch, :])
                    ins.then_inc(to_vector[g], c.adds(to_vector[g]))
                if j == 2:
                    out_projection(U0_SSD_OUT)
                pe.wait_ge(m_ready, c.want(m_ready, 2))
                g = grp()
                for ch in range(NC):
                    for e in range(2):
                        ins = mm(piece(g, ch, CH, SP_, e * SP_), XTOK[:, ch, e * SP_:(e + 1) * SP_],
                                 M[e][0:CH, ch * CH:(ch + 1) * CH])
                ins.then_inc(to_vector[g], c.adds(to_vector[g]))
                for d in range(2):
                    pe.wait_ge(st_ready, c.want(st_ready))
                    g = grp()
                    for ch in range(NC):
                        ins = mm(piece(g, ch, CH, P), ST[d][:, ch, :], chunk(CT, ch))
                    ins.then_inc(to_vector[g], c.adds(to_vector[g]))
            out_projection(U0_SSD_OUT + 2)
            assert gb[0] == b

        n = TILES_PER_GROUP
        with pe.Fori(0, GROUPS) as i, \
                c.rounds(GROUPS, i,
                         {staged: 1, bt_in: 16, ct_in: 16, xt_in: 16 * n, w_built: 2 * n, btok_ready: 1,
                          xw_ready: 2 * n, m_ready: 2 * n, st_ready: 2 * n, y_split: n, w_full[0]: 2,
                          w_full[1]: 2, grp_free[0]: 29, grp_free[1]: 29},
                         {w_free[0]: 2, w_free[1]: 2, to_scalar[b]: 13, to_scalar[b ^ 1]: 8, to_vector[b]: 16,
                          to_vector[b ^ 1]: 21}):
            scan_round()
        pe.wait_ge(sum_ready, c.want(sum_ready))
        sums_by_token(0, SS, one).then_inc(stat_full, c.adds(stat_full))
        spread_rms(b)
        b ^= 1
        b = feed_forward(U0_FFN1, b)
        pe.wait_ge(sum_ready, c.want(sum_ready))
        sums_by_token(0, SS, one).then_inc(stat_full, c.adds(stat_full))
        spread_rms(b)

    @block.scalar
    def _(act):
        c = Counts()
        sq_by = [None]

        def squares(src, done, dst=SQ):
            if sq_by[0] is not None:
                act.wait_ge(sq_by[0], c.want(sq_by[0]))
            act.activation(dst[:], src, ACT.Square).then_inc(sq_full, c.adds(sq_full))
            sq_by[0] = done

        def gain_and_squares(gain, ready):
            for k in range(KD):
                ready(k)
                act.activation(Uhi[:, k, :], H[:, k, :], ACT.Copy, scale=col(gain, k))\
                    .then_inc(hi_ready, c.adds(hi_ready))
                squares(H[:, k, :], sum_ready if k == KD - 1 else sq_free)

        def take_rms(b):
            act.wait_ge(to_scalar[b], c.want(to_scalar[b]))
            act.activation(banks(RMS[:]), group(b), ACT.Copy).then_inc(act_steps, c.adds(act_steps))
            act.wait_ge(act_steps, c.given(act_steps))
            act.sem_inc(grp_free[b], 1)
            act.sem_inc(rms_ready, 1)

        act.dma_start(cols[:], cols_d).then_inc(const_in, 16)
        act.dma_start(const[:], const_d).then_inc(const_in, 16)
        for k in range(KD):
            act.dma_start(H[:, k, :], x_d[k]).then_inc(x_in[k], 16)
        act.dma_start(trig_k, trig_d[2]).then_inc(trig_in, 16)
        for s in (*w_free, *grp_free):
            act.sem_inc(s, 1)
        act.sem_inc(ov_free, 2)

        act.wait_ge(const_in, c.want(const_in, 16 * 2))
        gain_and_squares("mix0", lambda k: act.wait_ge(x_in[k], c.want(x_in[k], 16)))
        for m in range(KQ + KKV):
            b = m % 2
            act.wait_ge(to_scalar[b], c.want(to_scalar[b]))
            if m >= 2:
                act.wait_ge(u_ready, c.want(u_ready, KD + 1 if m == 2 else 1))
            act.activation(banks(CF[b][:]), group(b), ACT.Copy).then_inc(act_steps, c.adds(act_steps))
            act.wait_ge(act_steps, c.given(act_steps))
            act.sem_inc(grp_free[b], 1)
            gain = col("q_norm", m) if m < KQ else col("kv_norm", m - KQ)
            act.activation(Chi[:, m, :], CF[b][:], ACT.Copy, scale=gain).then_inc(hi_ready, c.adds(hi_ready))
            squares(CF[b][:], sum_ready if m in (KQ - 1, KQ + KKV - 1) else sq_free)
        act.wait_ge(to_scalar[1], c.want(to_scalar[1]))
        act.wait_ge(u_ready, c.want(u_ready))
        act.activation(banks(CF[1][:]), group(1), ACT.Copy).then_inc(act_steps, c.adds(act_steps))
        act.wait_ge(act_steps, c.given(act_steps))
        act.sem_inc(grp_free[1], 1)
        act.wait_ge(sum_ready, c.want(sum_ready))
        act.activation(SQ[:], CF[1][:], ACT.Square).then_inc(rope_sq, c.adds(rope_sq))
        act.wait_ge(to_scalar[0], c.want(to_scalar[0]))
        act.activation(banks(KR[0][NOPE:P, :]), group(0, parts=P - NOPE, at=NOPE), ACT.Copy)\
            .then_inc(act_steps, c.adds(act_steps))
        act.activation(banks(KR[1][0:P - NOPE, :]), group(0, parts=P - NOPE), ACT.Copy)\
            .then_inc(grp_free[0], c.adds(grp_free[0]))
        sq_by[0] = None
        act.wait_ge(stat_full, c.want(stat_full))
        for k in range(2):
            act.dma_start(trig_q[:, k, :], trig_d[k]).then_inc(trig_in, 16)

        steps = [(h, s, t) for h in range(2) for s in range(NSEQ) for t in range(CS)]
        NS = len(steps)

        def attention_round(pair):
            for h in range(2):
                act.wait_ge(to_scalar[h], c.want(to_scalar[h]))
                act.activation(banks(QR[h][:]), group(h), ACT.Copy).then_inc(act_steps, c.adds(act_steps))
                act.wait_ge(act_steps, c.given(act_steps))
                act.sem_inc(grp_free[h], 1)
                act.activation(SQH[h][:], QR[h][:], ACT.Square).then_inc(q_squared, c.adds(q_squared))
            act.wait_ge(to_scalar[0], c.want(to_scalar[0]))
            act.activation(banks(KR[0][0:NOPE, :]), group(0, parts=NOPE), ACT.Copy,
                           scale=col("k_nope")[0:NOPE]).then_inc(act_steps, c.adds(act_steps))
            act.activation(banks(KR[1][NOPE:P, :]), group(0, parts=NOPE, at=NOPE), ACT.Copy,
                           scale=col("k_nope")[NOPE:P]).then_inc(act_steps, c.adds(act_steps))
            act.activation(banks(SQH[2][:]), group(0), ACT.Square).then_inc(act_steps, c.adds(act_steps))
            act.wait_ge(act_steps, c.given(act_steps))
            act.sem_inc(grp_free[0], 1)
            act.sem_inc(k_squared, 1)
            for n in range(NS + 2):
                if n < NS:
                    h, s, t = steps[n]
                    act.wait_ge(nb_ready, c.want(nb_ready))
                    ch = s * CS + t
                    act.activation(
               PR[n % 2][:].rearrange("p (j n) -> p j n", j=2),
               PS[0:CH, 2 * (n % 2):2 * (n % 2) + 2, 0:L // 2], ACT.Exp,
               bias=SMAX[:, n:n + 1], scale=STAT[:, S_QS + h, ch:ch + 1],
               accum_out=SSUM[:, n:n + 1]).then_inc(p_full, c.adds(p_full))
                if n >= 2:
                    h, s, t = steps[n - 2]
                    act.wait_ge(ov_full, c.want(ov_full))
                    act.wait_ge(rinv_ready, c.want(rinv_ready))
                    act.activation(O[:, s * CS + t, h * VD:(h + 1) * VD], PS[0:CH, 6 + n % 2, 0:VD],
                                   ACT.Copy, scale=SINV[:, n - 2:n - 1]).then_inc(ov_free, c.adds(ov_free))
            act.wait_ge(to_scalar[0], c.want(to_scalar[0]))
            act.activation(H[:, bass.ds(pair, 1), :].rearrange("p o (b n) -> p (o b) n", b=NB),
                           group(0), ACT.Copy).then_inc(act_steps, c.adds(act_steps))
            act.wait_ge(act_steps, c.given(act_steps))
            act.sem_inc(grp_free[0], 1)

        with act.Fori(0, PAIRS) as pair, \
                c.rounds(PAIRS, pair,
                         {to_scalar[0]: 3, to_scalar[1]: 1, nb_ready: NS, ov_full: NS, rinv_ready: NS},
                         {act_steps: 6, p_full: NS, ov_free: NS, q_squared: 2}):
            attention_round(pair)

        for k in range(KD):
            act.activation(Ohi[:, k, :], H[:, k, :], ACT.Copy).then_inc(hi_ready, c.adds(hi_ready))
        act.wait_ge(o_split, c.want(o_split, KD))
        act.wait_ge(hi_ready, c.given(hi_ready))
        for k in range(KD):
            act.dma_start(H[:, k, :], x_d[k]).then_inc(x_in[k], 16)
        gain_and_squares("ffn0", lambda k: act.wait_ge(h_ready, c.want(h_ready)))

        def feed_forward(b):
            take_rms(b)

            def silu():
                act.wait_ge(gate_ready, c.want(gate_ready))
                act.activation(SILU[:], GATE[:], ACT.Silu).then_inc(silu_ready, c.adds(silu_ready))

            def split(k):
                act.wait_ge(hid_ready, c.want(hid_ready))
                act.activation(HIDhi[:, k, :], HID[:], ACT.Copy).then_inc(hid_hi, c.adds(hid_hi))

            for k in range(F_STEP):
                silu()
                split(k)
            with act.Fori(0, F_STEPS - 1) as i, \
                    c.rounds(F_STEPS - 1, i,
                             {gate_ready: F_STEP, hid_ready: F_STEP},
                             {silu_ready: F_STEP, hid_hi: F_STEP}):
                for k in range(F_STEP):
                    silu()
                    split(k)

        feed_forward(1)
        gain_and_squares("mix1", lambda k: act.wait_ge(h_ready, c.want(h_ready)))
        act.dma_start(ROWS[:].rearrange("p a d h -> p a (d h)"), rows_d).then_inc(rows_in, 16)
        act.wait_ge(hi_ready, c.given(hi_ready))
        for k in range(KD):
            act.dma_start(h_d[k], H[:, k, :]).then_inc(h_saved, 16)
        for k in range(2):
            act.sem_inc(yc_out[k], 16)
        act.sem_inc(w_read, 1)
        take_rms(0)

        def silu_out(n, dram):
            with act.Fori(0, n // 2) as i, \
                    c.rounds(n // 2, i,
                             {yc_ready: 2},
                             {act_steps: 2}):
                for k in range(2):
                    act.wait_ge(yc_ready, c.want(yc_ready))
                    act.activation(YC[k][:], YC[k][:], ACT.Silu).then_inc(act_steps, c.adds(act_steps))
                    act.wait_ge(act_steps, c.given(act_steps))
                    act.dma_start(dram[bass.ds(i * 2 + k, 1)].rearrange("o p t -> p (o t)"), YC[k][:])\
                       .then_inc(yc_out[k], 16)

        silu_out(CONV_TILES, xbc_d)
        act.wait_ge(rows_in, c.want(rows_in, 16))
        act.activation(ROWS[:, 1], ROWS[:, 1], ACT.Exp).then_inc(exp_out, c.adds(exp_out))
        act.wait_ge(exp_in, c.want(exp_in))
        act.activation(E1[:], E1[:], ACT.Exp, scale=-1.0).then_inc(exp_out, c.adds(exp_out))
        silu_out(Z_TILES, z_d)
        act.wait_ge(exp_in, c.want(exp_in))
        act.activation(WST[:], WST[:], ACT.Exp).then_inc(exp_out, c.adds(exp_out))
        act.activation(DECAY[:], DECAY[:], ACT.Exp).then_inc(exp_out, c.adds(exp_out))

        act.wait_ge(sum_ready, c.want(sum_ready))
        sq_by[0] = None
        for k in range(2):
            act.wait_ge(yc_out[k], 16 * (1 + (CONV_TILES + Z_TILES) // 2))
        act.wait_ge(scan_free, c.want(scan_free))
        act.dma_start(XT[:], xbc_d[0]).then_inc(xt_in, 16)

        def scan_round(i):
            gb = [B_SCAN]

            def grp():
                gb[0] ^= 1
                return gb[0] ^ 1

            def take(dst, src_parts, func, width, parts, *also):
                g = grp()
                act.wait_ge(to_scalar[g], c.want(to_scalar[g]))
                act.activation(dst, group(g, CB * width, parts), func).then_inc(act_steps, c.adds(act_steps))
                act.wait_ge(act_steps, c.given(act_steps))
                act.sem_inc(grp_free[g], 1)
                for s in also:
                    act.sem_inc(s, 1)

            def tile_in(dst, dram, index, sem_in):
                act.dma_start(dst[:], dram[bass.ds(index, 1)].rearrange("o p t -> p (o t)")).then_inc(sem_in, 16)

            for j in range(TILES_PER_GROUP):
                act.wait_ge(sq_free, c.want(sq_free))
                if j == 0:
                    tile_in(BT, xbc_d, i + Z_TILES, bt_in)
                    tile_in(CT, xbc_d, i + (Z_TILES + GROUPS), ct_in)
                tile_in(ZT, z_d, i * TILES_PER_GROUP + j, zt_in)
                if j == 0:
                    act.wait_ge(staged, c.want(staged))
                    take(BTOK[:].rearrange("p (b c) n -> p b (c n)", b=NB), None, ACT.Copy, P, CH, btok_ready)
                    grp()
                take(XTOK[:].rearrange("p (b c) n -> p b (c n)", b=NB), None, ACT.Copy, P, CH, xtok_ready)
                act.activation(Y[:], XT[:], ACT.Copy, scale=SKIPG[:, j:j + 1]).then_inc(y0_ready, c.adds(y0_ready))
                take(banks(M[0][0:CH, :]), None, ACT.Exp, CH, CH, w_read, l_ready)
                act.wait_ge(y0_ready, c.given(y0_ready))
                tile_in(XT, xbc_d, i * TILES_PER_GROUP + (j + 1), xt_in)
                take(banks(EB[0][:]), None, ACT.Exp, CH, P, eb_ready)
                take(banks(EB[1][:]), None, ACT.Exp, CH, P, eb_ready)
                take(banks(M[1][0:CH, :]), None, ACT.Exp, CH, CH, w_read, l_ready)
                gb[0] ^= 1
                act.wait_ge(y_ready, c.want(y_ready))
                act.activation(Yhi[:, j % 2, :], Y[:], ACT.Copy, scale=NORMG[:, j:j + 1]).then_inc(y_hi, c.adds(y_hi))
                act.activation(SQ[:], Y[:], ACT.Square).then_inc(sq_full, c.adds(sq_full))

        n = TILES_PER_GROUP
        with act.Fori(0, GROUPS) as i, \
                c.rounds(GROUPS, i,
                         {sq_free: n, staged: 1, to_scalar[B_SCAN]: 13, to_scalar[B_SCAN ^ 1]: 8, y_ready: n},
                         {act_steps: 1 + 5 * n, y0_ready: n, y_hi: n, sq_full: n}):
            scan_round(i)
        act.wait_ge(sum_ready, c.want(sum_ready))
        act.wait_ge(sq_free, c.want(sq_free))
        act.wait_ge(xt_in, 16 * (Z_TILES + 1))
        take_rms(B_SCAN)
        for k in range(2):
            act.dma_start(M[k][:], h_d[k]).then_inc(h_back[k % 2], 16)

        def mixed(k):
            act.wait_ge(h_ready, c.want(h_ready))
            if k + 2 < KD:
                act.dma_start(M[k % 2][:], h_d[k + 2]).then_inc(h_back[k % 2], 16)

        gain_and_squares("ffn1", mixed)
        feed_forward(B_FFN1)
        for k in range(KD):
            act.wait_ge(h_ready, c.want(h_ready))
            squares(H[:, k, :], sum_ready if k == KD - 1 else sq_free)
        take_rms(B_LAST)
        for k in range(KD):
            act.wait_ge(out_ready, c.want(out_ready))
            act.dma_start(out_d[k], H[:, k, :]).then_inc(out_done, 16)
        act.wait_ge(out_done, 16 * KD)

    @block.vector
    def _(vec):
        c = Counts()

        def add_squares(dst, first, last):
            vec.wait_ge(sq_full, c.want(sq_full))
            if first:
                ins = vec.tensor_copy(dst[:], SQ[:])
            else:
                vec.wait_ge(sq_free, c.given(sq_free))
                ins = vec.tensor_tensor(dst[:], dst[:], SQ[:], ALU.add)
            ins.then_inc(sum_ready if last else sq_free, c.adds(sum_ready if last else sq_free))

        def wait_grp(gb):
            gb[0] ^= 1
            return gb[0] ^ 1

        def lo_part(k, gain, ready=None):
            if ready:
                ready(k)
            vec.wait_ge(hi_ready, c.want(hi_ready))
            vec.scalar_tensor_tensor(Ulo[:, k, :], H[:, k, :], col(gain, k), Uhi[:, k, :].bitcast(F32),
                                     ALU.mult, ALU.subtract).then_inc(u_ready, c.adds(u_ready))
            add_squares(SS, k == 0, k == KD - 1)

        def rsqrt(y, v):
            tmp = STAT[:, S_TMP:S_TMP + 2, :] if len(y.shape) == 3 else stat(S_TMP)
            vec.tensor_scalar(y.bitcast(I32), v.bitcast(I32), 1, None, ALU.logical_shift_right)\
                .then_inc(vec_steps, c.adds(vec_steps))
            vec.wait_ge(vec_steps, c.given(vec_steps))
            vec.tensor_scalar(y.bitcast(I32), y.bitcast(I32), -1.0, float(0x5F3759DF), ALU.mult, ALU.add)\
                .then_inc(vec_steps, c.adds(vec_steps))
            vec.wait_ge(vec_steps, c.given(vec_steps))
            for _ in range(3):
                vec.tensor_tensor(tmp, y, y, ALU.mult).then_inc(vec_steps, c.adds(vec_steps))
                vec.wait_ge(vec_steps, c.given(vec_steps))
                vec.scalar_tensor_tensor(tmp, tmp, -0.5, v, ALU.mult, ALU.mult).then_inc(vec_steps, c.adds(vec_steps))
                vec.wait_ge(vec_steps, c.given(vec_steps))
                vec.scalar_tensor_tensor(y, tmp, 1.5, y, ALU.add, ALU.mult).then_inc(vec_steps, c.adds(vec_steps))
                vec.wait_ge(vec_steps, c.given(vec_steps))

        def stat_sum(k, n=1):
            ap = PS[0:CH, STAT_BANK, k * NC:(k + n) * NC]
            return ap if n == 1 else ap.rearrange("p (k c) -> p k c", c=NC)

        def rms_factor(width):
            vec.wait_ge(stat_full, c.want(stat_full))
            vec.tensor_scalar(stat(S_V), stat_sum(0), 1.0 / width, EPS, ALU.mult, ALU.add)\
                .then_inc(vec_steps, c.adds(vec_steps))
            vec.wait_ge(vec_steps, c.given(vec_steps))
            rsqrt(stat(S_R1), stat(S_V))
            vec.sem_inc(row_ready, 1)

        vec.wait_ge(const_in, c.want(const_in, 16 * 2))
        for k in range(KD):
            lo_part(k, "mix0", lambda k: vec.wait_ge(x_in[k], c.want(x_in[k], 16)))
        for m in range(KQ + KKV):
            vec.wait_ge(hi_ready, c.want(hi_ready))
            gain = col("q_norm", m) if m < KQ else col("kv_norm", m - KQ)
            vec.scalar_tensor_tensor(Clo[:, m, :], CF[m % 2][:], gain, Chi[:, m, :].bitcast(F32),
                                     ALU.mult, ALU.subtract).then_inc(u_ready, c.adds(u_ready))
            add_squares(SSQ[m >= KQ], m in (0, KQ), m in (KQ - 1, KQ + KKV - 1))
        vec.wait_ge(rope_sq, c.want(rope_sq))
        vec.wait_ge(trig_in, c.want(trig_in, 16))
        vec.wait_ge(u_ready, c.given(u_ready))
        vec.scalar_tensor_tensor(seqs(CF[0][:]), seqs(CF[1][:]), col("k_rope"),
                                 trig_k.unsqueeze(1).broadcast_to([P, NSEQ, L]),
                                 ALU.mult, ALU.mult).then_inc(rope_ready, c.adds(rope_ready))
        vec.wait_ge(stat_full, c.want(stat_full))
        vec.tensor_scalar(stat(S_V), stat_sum(0), 1.0 / D_MODEL, EPS, ALU.mult, ALU.add)\
            .then_inc(vec_steps, c.adds(vec_steps))
        vec.wait_ge(vec_steps, c.given(vec_steps))
        rsqrt(stat(S_R1), stat(S_V))
        vec.tensor_tensor(stat(S_R1SQ), stat(S_R1), stat(S_R1), ALU.mult).then_inc(vec_steps, c.adds(vec_steps))
        vec.wait_ge(vec_steps, c.given(vec_steps))
        for k, (rank, dst, dst2) in enumerate(((Q_RANK, S_A, S_A2), (KV_RANK, S_B, S_B2))):
            vec.scalar_tensor_tensor(stat(S_V), stat_sum(1 + k), 1.0 / rank, stat(S_R1SQ), ALU.mult, ALU.mult)\
                .then_inc(vec_steps, c.adds(vec_steps))
            vec.wait_ge(vec_steps, c.given(vec_steps))
            vec.tensor_scalar(stat(S_V), stat(S_V), EPS, None, ALU.add).then_inc(vec_steps, c.adds(vec_steps))
            vec.wait_ge(vec_steps, c.given(vec_steps))
            rsqrt(stat(dst), stat(S_V))
            vec.tensor_tensor(stat(dst), stat(dst), stat(S_R1), ALU.mult).then_inc(vec_steps, c.adds(vec_steps))
            vec.wait_ge(vec_steps, c.given(vec_steps))
            vec.scalar_tensor_tensor(stat(dst2), stat(dst), 1.0 / QK, stat(dst), ALU.mult, ALU.mult)\
                .then_inc(vec_steps, c.adds(vec_steps))
            vec.wait_ge(vec_steps, c.given(vec_steps))
        vec.scalar_tensor_tensor(stat(S_RR), stat_sum(3), 1.0 / QK, stat(S_R1SQ), ALU.mult, ALU.mult)\
            .then_inc(vec_steps, c.adds(vec_steps))
        vec.wait_ge(vec_steps, c.given(vec_steps))
        vec.sem_inc(row_ready, 1)
        vec.tensor_scalar(stat(S_RR), stat(S_RR), EPS, None, ALU.add).then_inc(vec_steps, c.adds(vec_steps))
        vec.wait_ge(vec_steps, c.given(vec_steps))
        vec.wait_ge(trig_in, c.want(trig_in, 32))
        for h in range(2):
            vec.tensor_scalar(trig_q[:, h, :], trig_q[:, h, :], col("q_head", h), None, ALU.mult)\
                .then_inc(vec_steps, c.adds(vec_steps))
            vec.wait_ge(vec_steps, c.given(vec_steps))

        steps = [(h, s, t) for h in range(2) for s in range(NSEQ) for t in range(CS)]
        NS = len(steps)

        def both(k):
            return stat(k).unsqueeze(1).broadcast_to([CH, 2, NC])

        def attention_round():
            vec.wait_ge(to_vector[1], c.want(to_vector[1]))
            vec.tensor_tensor(V[:].rearrange("p (b c) d -> p b c d", b=NB),
                             group(1, CB * P, CH).rearrange("p b (c d) -> p b c d", d=P),
                             stat(S_B).rearrange("p (b c) -> p b c", b=NB).unsqueeze(3)
                             .broadcast_to([CH, NB, CB, P]), ALU.mult).then_inc(vec_steps, c.adds(vec_steps))
            vec.wait_ge(vec_steps, c.given(vec_steps))
            vec.sem_inc(grp_free[1], 1)
            vec.sem_inc(v_ready, 1)
            vec.wait_ge(stat_full, c.want(stat_full))
            for h in range(2):
                vec.tensor_tensor(seqs(Q[h][:]), seqs(QR[h][:]),
                                  trig_q[:, h, :].unsqueeze(1).broadcast_to([P, NSEQ, L]), ALU.mult)\
                    .then_inc(q_ready, c.adds(q_ready))
            v2, y2 = stat(S_V, 2), stat(S_QS, 2)
            vec.tensor_tensor(v2, stat_sum(0, 2), both(S_A2), ALU.mult).then_inc(vec_steps, c.adds(vec_steps))
            vec.wait_ge(vec_steps, c.given(vec_steps))
            vec.tensor_scalar(v2, v2, EPS, None, ALU.add).then_inc(vec_steps, c.adds(vec_steps))
            vec.wait_ge(vec_steps, c.given(vec_steps))
            rsqrt(y2, v2)
            vec.scalar_tensor_tensor(y2, y2, 1.0 / math.sqrt(QK), both(S_A), ALU.mult, ALU.mult)\
                .then_inc(vec_steps, c.adds(vec_steps))
            vec.wait_ge(vec_steps, c.given(vec_steps))
            vec.tensor_tensor(v2, stat_sum(2, 2), both(S_B2), ALU.mult).then_inc(vec_steps, c.adds(vec_steps))
            vec.wait_ge(vec_steps, c.given(vec_steps))
            vec.tensor_tensor(v2, v2, both(S_RR), ALU.add).then_inc(vec_steps, c.adds(vec_steps))
            vec.wait_ge(vec_steps, c.given(vec_steps))
            rsqrt(stat(S_KF, 2), v2)
            for h in range(2):
                for part, f in ((0, S_B), (1, S_R1)):
                    vec.tensor_tensor(KS[:, :, 2 * h + (part ^ h)], stat(S_KF + h), stat(f), ALU.mult)\
                        .then_inc(vec_steps, c.adds(vec_steps))
            vec.wait_ge(vec_steps, c.given(vec_steps))
            vec.sem_inc(ks_ready, 1)
            for h in range(2):
                vec.wait_ge(to_vector[h], c.want(to_vector[h]))
                vec.tensor_tensor(banks(KM[h][:]), banks(KR[h][:]), group(h), ALU.mult)\
                    .then_inc(vec_steps, c.adds(vec_steps))
                vec.wait_ge(vec_steps, c.given(vec_steps))
                vec.sem_inc(grp_free[h], 1)
                vec.sem_inc(km_ready, 1)
            for n in range(NS + 1):
                if n < NS:
                    h, s, t = steps[n]
                    ch = s * CS + t
                    vec.wait_ge(sc_full, c.want(sc_full))
                    vec.tensor_reduce(SMAX[:, n:n + 1], PS[0:CH, 2 * (n % 2):2 * (n % 2) + 2, 0:L // 2],
                                      AX_XY, ALU.max).then_inc(vec_steps, c.adds(vec_steps))
                    vec.wait_ge(vec_steps, c.given(vec_steps))
                    vec.tensor_scalar(SMAX[:, n:n + 1], SMAX[:, n:n + 1], STAT[:, S_QS + h, ch:ch + 1],
                                      -1.0, ALU.mult, ALU.mult).then_inc(nb_ready, c.adds(nb_ready))
                if n >= 1:
                    vec.wait_ge(pt_full, c.want(pt_full))
                    vec.tensor_copy(PT[(n - 1) % 2][:].rearrange("p (j k) q -> p j (k q)", j=2),
                                    PS[0:CH, 4:6, 0:L // 2]).then_inc(pt_ready, c.adds(pt_ready))
                    vec.reciprocal(SINV[:, n - 1:n], SSUM[:, n - 1:n]).then_inc(rinv_ready, c.adds(rinv_ready))

        with vec.Fori(0, PAIRS) as i, \
                c.rounds(PAIRS, i,
                         {to_vector[0]: 1, to_vector[1]: 2, stat_full: 1, sc_full: NS, pt_full: NS},
                         {vec_steps: 1 + 2 + 11 + 1 + 2 + 11 + 4 + 2 + NS, q_ready: 2, nb_ready: NS,
                          pt_ready: NS, rinv_ready: NS}):
            attention_round()

        for k in range(KD):
            vec.wait_ge(hi_ready, c.want(hi_ready))
            vec.tensor_tensor(Olo[:, k, :], H[:, k, :], Ohi[:, k, :].bitcast(F32), ALU.subtract)\
                .then_inc(o_split, c.adds(o_split))

        def add_to_h(m, b, final):
            vec.wait_ge(to_vector[b], c.want(to_vector[b]))
            ins = vec.tensor_tensor(banks(H[:, m, :]), banks(H[:, m, :]), group(b), ALU.add)
            if final:
                ins.then_inc(vec_steps, c.adds(vec_steps))
                vec.wait_ge(vec_steps, c.given(vec_steps))
                vec.sem_inc(grp_free[b], 1)
                vec.sem_inc(h_ready, 1)
            else:
                ins.then_inc(grp_free[b], c.adds(grp_free[b]))

        for m in range(KD):
            vec.wait_ge(x_in[m], c.want(x_in[m], 16))
            add_to_h(m, m % 2, True)
            lo_part(m, "ffn0")

        def feed_forward(b0, after):
            b = [b0]

            def grp():
                b[0] ^= 1
                return b[0] ^ 1

            def gate(g):
                vec.wait_ge(to_vector[g], c.want(to_vector[g]))
                vec.tensor_tensor(banks(GATE[:]), group(g), banks(RMS[:]), ALU.mult)\
                    .then_inc(vec_steps, c.adds(vec_steps))
                vec.wait_ge(vec_steps, c.given(vec_steps))
                vec.sem_inc(grp_free[g], 1)
                vec.sem_inc(gate_ready, 1)

            def up(g, k):
                vec.wait_ge(to_vector[g], c.want(to_vector[g]))
                vec.tensor_tensor(banks(HID[:]), group(g), banks(RMS[:]), ALU.mult)\
                    .then_inc(vec_steps, c.adds(vec_steps))
                vec.wait_ge(vec_steps, c.given(vec_steps))
                vec.sem_inc(grp_free[g], 1)
                vec.wait_ge(silu_ready, c.want(silu_ready))
                vec.tensor_tensor(HID[:], HID[:], SILU[:], ALU.mult).then_inc(hid_ready, c.adds(hid_ready))
                vec.wait_ge(hid_hi, c.want(hid_hi))
                vec.wait_ge(hid_ready, c.given(hid_ready))
                vec.tensor_tensor(HIDlo[:, k, :], HID[:], HIDhi[:, k, :].bitcast(F32), ALU.subtract)\
                    .then_inc(hid_split, c.adds(hid_split))

            g0 = grp()
            rms_factor(D_MODEL)
            grp()
            vec.wait_ge(rms_ready, c.want(rms_ready))
            gate(g0)
            up(grp(), 0)
            gate(grp())
            up(grp(), 1)
            with vec.Fori(0, F_STEPS - 1) as i, \
                    c.rounds(F_STEPS - 1, i,
                             {to_vector[0]: 6, to_vector[1]: 6, silu_ready: F_STEP, hid_hi: F_STEP},
                             {vec_steps: 2 * F_STEP, hid_ready: F_STEP, hid_split: F_STEP, grp_free[0]: 4,
                              grp_free[1]: 4}):
                gate(grp())
                for m in range(KD):
                    add_to_h(m, grp(), False)
                up(grp(), 0)
                gate(grp())
                up(grp(), 1)
            for m in range(KD):
                add_to_h(m, grp(), True)
                after(m)
            return b[0]

        b = feed_forward(0, lambda m: lo_part(m, "mix1"))

        rms_factor(D_MODEL)
        vec.wait_ge(to_vector[b], c.want(to_vector[b]))
        for d in range(2):
            ins = vec.tensor_tensor(
                DT[:, d].rearrange("p (b c) h -> p b c h", b=NB),
                group(b, CB * 2 * SHEADS, CH).rearrange("p b (c n) -> p b c n", c=CB)[..., d * SHEADS:(d + 1) * SHEADS],
                stat(S_R1).rearrange("p (b c) -> p b c", b=NB).unsqueeze(3).broadcast_to([CH, NB, CB, SHEADS]),
                ALU.mult)
            if d:
                ins.then_inc(vec_steps, c.adds(vec_steps))
                vec.wait_ge(vec_steps, c.given(vec_steps))
                vec.sem_inc(grp_free[b], 1)
            else:
                ins.then_inc(vec_steps, c.adds(vec_steps))
        vec.wait_ge(rms_ready, c.want(rms_ready))

        def conv(tile, k):
            vec.tensor_copy(TAPS[:], cols[:, bass.ds(tile * (D_CONV + 1) + COLS["conv"], D_CONV + 1)])\
                .then_inc(vec_steps, c.adds(vec_steps))
            vec.wait_ge(vec_steps, c.given(vec_steps))
            x, y, mid = seqs(XC[:]), seqs(YC[k][:]), D_CONV // 2
            vec.tensor_scalar(y, x, TAPS[:, mid:mid + 1], TAPS[:, D_CONV:D_CONV + 1], ALU.mult, ALU.add)\
                .then_inc(vec_steps, c.adds(vec_steps))
            vec.wait_ge(vec_steps, c.given(vec_steps))
            for tap in (0, 1, 3, 4):
                off = tap - mid
                to = slice(max(0, -off), L - max(0, off))
                of = slice(max(0, off), L - max(0, -off))
                ins = vec.scalar_tensor_tensor(y[:, :, to], x[:, :, of], TAPS[:, tap:tap + 1], y[:, :, to],
                                               ALU.mult, ALU.add)
                ins.then_inc(vec_steps, c.adds(vec_steps))
                vec.wait_ge(vec_steps, c.given(vec_steps))
            vec.sem_inc(yc_ready, 1)

        with vec.Fori(0, CONV_TILES // 2) as i, \
                c.rounds(CONV_TILES // 2, i,
                         {to_vector[0]: 1, to_vector[1]: 1, yc_out[0]: 16, yc_out[1]: 16},
                         {vec_steps: 2 * 7}):
            for k, g in ((0, b), (1, b ^ 1)):
                vec.wait_ge(to_vector[g], c.want(to_vector[g]))
                vec.tensor_tensor(banks(XC[:]), group(g), banks(RMS[:]), ALU.mult)\
                    .then_inc(vec_steps, c.adds(vec_steps))
                vec.wait_ge(vec_steps, c.given(vec_steps))
                vec.sem_inc(grp_free[g], 1)
                vec.wait_ge(yc_out[k], c.want(yc_out[k], 16))
                conv(i * 2 + k, k)

        vec.wait_ge(exp_out, c.want(exp_out))
        vec.tensor_tensor(DT[:], DT[:], ROWS[:, 0].unsqueeze(2).broadcast_to([CH, 2, NC, SHEADS]), ALU.add)\
            .then_inc(vec_steps, c.adds(vec_steps))
        vec.wait_ge(vec_steps, c.given(vec_steps))
        vec.scalar_tensor_tensor(E1[:], DT[:], -1.0, DT[:], ALU.mult, ALU.max).then_inc(exp_in, c.adds(exp_in))
        vec.tensor_scalar(DT[:], DT[:], 0.0, None, ALU.max).then_inc(vec_steps, c.adds(vec_steps))
        vec.wait_ge(vec_steps, c.given(vec_steps))
        vec.wait_ge(exp_out, c.want(exp_out))
        vec.tensor_scalar(E2[:], E1[:], 2.0, None, ALU.add).then_inc(vec_steps, c.adds(vec_steps))
        vec.wait_ge(vec_steps, c.given(vec_steps))
        vec.reciprocal(E2[:], E2[:]).then_inc(vec_steps, c.adds(vec_steps))
        vec.wait_ge(vec_steps, c.given(vec_steps))
        vec.tensor_tensor(E2[:], E1[:], E2[:], ALU.mult).then_inc(vec_steps, c.adds(vec_steps))
        vec.wait_ge(vec_steps, c.given(vec_steps))
        vec.tensor_tensor(E1[:], E2[:], E2[:], ALU.mult).then_inc(vec_steps, c.adds(vec_steps))
        vec.wait_ge(vec_steps, c.given(vec_steps))
        vec.tensor_scalar(E3[:], E1[:], 1.0 / 15, None, ALU.mult).then_inc(vec_steps, c.adds(vec_steps))
        vec.wait_ge(vec_steps, c.given(vec_steps))
        for k in (13, 11, 9, 7, 5, 3):
            vec.scalar_tensor_tensor(E3[:], E3[:], 1.0 / k, E1[:], ALU.add, ALU.mult)\
                .then_inc(vec_steps, c.adds(vec_steps))
            vec.wait_ge(vec_steps, c.given(vec_steps))
        vec.scalar_tensor_tensor(E3[:], E3[:], 1.0, E2[:], ALU.add, ALU.mult).then_inc(vec_steps, c.adds(vec_steps))
        vec.wait_ge(vec_steps, c.given(vec_steps))
        vec.scalar_tensor_tensor(DT[:], E3[:], 2.0, DT[:], ALU.mult, ALU.add).then_inc(vec_steps, c.adds(vec_steps))
        vec.wait_ge(vec_steps, c.given(vec_steps))
        for d in range(2):
            vec.scalar_tensor_tensor(A[:, d], DT[:, d], -1.0,
                                     ROWS[:, 1, d].unsqueeze(1).broadcast_to([CH, NC, SHEADS]),
                                     ALU.mult, ALU.mult).then_inc(vec_steps, c.adds(vec_steps))
        vec.wait_ge(vec_steps, c.given(vec_steps))
        vec.sem_inc(a_ready, 1)

        with vec.Fori(0, Z_TILES // 2) as i, \
                c.rounds(Z_TILES // 2, i,
                         {to_vector[0]: 1, to_vector[1]: 1, yc_out[0]: 16, yc_out[1]: 16},
                         {vec_steps: 2}):
            for k, g in ((0, b), (1, b ^ 1)):
                vec.wait_ge(yc_out[k], c.want(yc_out[k], 16))
                vec.wait_ge(to_vector[g], c.want(to_vector[g]))
                vec.tensor_tensor(banks(YC[k][:]), group(g), banks(RMS[:]), ALU.mult)\
                    .then_inc(vec_steps, c.adds(vec_steps))
                vec.wait_ge(vec_steps, c.given(vec_steps))
                vec.sem_inc(grp_free[g], 1)
                vec.sem_inc(yc_ready, 1)
        vec.wait_ge(to_vector[b], c.want(to_vector[b]))
        vec.tensor_copy(CSUM[:].rearrange("p d c h -> p d (c h)"),
                        PS[0:CH, NB * b:NB * b + 2, 0:NC * SHEADS]).then_inc(vec_steps, c.adds(vec_steps))
        vec.wait_ge(vec_steps, c.given(vec_steps))
        vec.sem_inc(grp_free[b], 1)
        g = b ^ 1
        vec.wait_ge(to_vector[g], c.want(to_vector[g]))
        vec.tensor_copy(DECAY[:].rearrange("p d c h -> p d (c h)"),
                        PS[:, NB * g:NB * g + 2, 0:NC * SHEADS]).then_inc(vec_steps, c.adds(vec_steps))
        vec.wait_ge(vec_steps, c.given(vec_steps))
        vec.sem_inc(grp_free[g], 1)
        vec.sem_inc(scan_free, 1)
        vec.tensor_tensor(WST[:], DECAY[0:CH], CSUM[:], ALU.subtract).then_inc(exp_in, c.adds(exp_in))
        vec.wait_ge(h_saved, c.want(h_saved, 16 * KD))
        vec.memset(H[:], 0.0).then_inc(vec_steps, c.adds(vec_steps))
        for k in range(2):
            vec.wait_ge(yc_out[k], c.ahead(yc_out[k], 16))
        for d in range(2):
            vec.memset(ST[d][:], 0.0).then_inc(vec_steps, c.adds(vec_steps))
        vec.memset(SS[:], 0.0).then_inc(sq_free, c.adds(sq_free))
        vec.wait_ge(exp_out, c.want(exp_out, 2))
        vec.tensor_tensor(WST[:], WST[:], DT[:], ALU.mult).then_inc(vec_steps, c.adds(vec_steps))
        vec.wait_ge(vec_steps, c.given(vec_steps))

        def scan_round(i):
            gb = [b]

            def grp():
                gb[0] ^= 1
                vec.wait_ge(to_vector[gb[0] ^ 1], c.want(to_vector[gb[0] ^ 1]))
                return gb[0] ^ 1

            def skip():
                gb[0] ^= 1

            def over(ap, n):
                return ap.unsqueeze(2).broadcast_to([ap.shape[0], NC, n])

            for src, dst in ((A, AG), (DT, DTG), (WST, WG), (DECAY, DECG)):
                vec.tensor_copy(dst[:], src[:, :, :, bass.ds(i * HPG, HPG)]).then_inc(vec_steps, c.adds(vec_steps))
            for name, dst in (("skip", SKIPG), ("ssd_norm", NORMG)):
                vec.tensor_copy(dst[:], cols[:, bass.ds(i * TILES_PER_GROUP + COLS[name], TILES_PER_GROUP)])\
                    .then_inc(vec_steps, c.adds(vec_steps))
            vec.wait_ge(vec_steps, c.given(vec_steps))
            vec.sem_inc(staged, 1)
            skip()
            g = grp()
            gv = group(g, CB * CH, CH).rearrange("p b (c t) -> p b c t", t=CH)
            for d, m in ((0, upper), (1, lower)):
                ins = vec.tensor_tensor(G[d][:].rearrange("p (b c) t -> p b c t", b=NB), gv,
                                        m.unsqueeze(1).unsqueeze(1).broadcast_to([CH, NB, CB, CH]), ALU.mult)
                if d:
                    ins.then_inc(vec_steps, c.adds(vec_steps))
                    vec.wait_ge(vec_steps, c.given(vec_steps))
                    vec.sem_inc(grp_free[g], 1)
                else:
                    ins.then_inc(vec_steps, c.adds(vec_steps))
            for j in range(TILES_PER_GROUP):
                h = 2 * j
                vec.wait_ge(xtok_ready, c.want(xtok_ready))
                for d in range(2):
                    for e in range(2):
                        ins = vec.tensor_tensor(XW[d][:, :, e * SP_:(e + 1) * SP_],
                                                XTOK[:, :, e * SP_:(e + 1) * SP_], over(dcol(WG, d, h + e), SP_),
                                                ALU.mult)
                        if e:
                            ins.then_inc(xw_ready, c.adds(xw_ready))
                        else:
                            ins.then_inc(vec_steps, c.adds(vec_steps))
                t2 = T2[0:CH].rearrange("p (c t) -> p c t", t=CH)
                for e in range(2):
                    vec.tensor_tensor(TM[:], G[0][:], over(dcol(DTG, 0, h + e), CH), ALU.mult)\
                        .then_inc(vec_steps, c.adds(vec_steps))
                    vec.tensor_tensor(t2, G[1][:], over(dcol(DTG, 1, h + e), CH), ALU.mult)\
                        .then_inc(vec_steps, c.adds(vec_steps))
                    vec.wait_ge(vec_steps, c.given(vec_steps))
                    vec.tensor_tensor(TM[:], TM[:], t2, ALU.add).then_inc(vec_steps, c.adds(vec_steps))
                    vec.wait_ge(vec_steps, c.given(vec_steps))
                    vec.wait_ge(l_ready, c.want(l_ready))
                    m = chunks(M[e][0:CH, :])
                    vec.tensor_tensor(m, m, TM[:], ALU.mult).then_inc(vec_steps, c.adds(vec_steps))
                    vec.wait_ge(vec_steps, c.given(vec_steps))
                    vec.sem_inc(m_ready, 1)
                for _ in range(5):
                    skip()
                for d in range(2):
                    g = grp()
                    new = PS[:, NB * g:NB * g + NB, :].rearrange("p b n -> p (b n)")\
                        .rearrange("p (s c e n) -> p s c e n", s=NSEQ, c=CS, e=2)
                    state = ST[d][:].rearrange("p (s c) (e n) -> p s c e n", s=NSEQ, e=2)
                    decay = DECG[:, d].rearrange("p (s c) h -> p s c h", s=NSEQ)
                    for k in range(CS - 1):
                        at, to = (k, k + 1) if d == 0 else (CS - 1 - k, CS - 2 - k)
                        vec.tensor_tensor(CARRY[:], state[:, :, at], decay[:, :, at, h:h + 2].unsqueeze(3)
                                          .broadcast_to([P, NSEQ, 2, SP_]), ALU.mult)\
                            .then_inc(vec_steps, c.adds(vec_steps))
                        vec.wait_ge(vec_steps, c.given(vec_steps))
                        vec.tensor_tensor(state[:, :, to], CARRY[:], new[:, :, at], ALU.add)\
                            .then_inc(vec_steps, c.adds(vec_steps))
                        vec.wait_ge(vec_steps, c.given(vec_steps))
                    vec.sem_inc(st_ready, 1)
                    vec.sem_inc(grp_free[g], 1)
                if j == 2:
                    for m in range(KD):
                        add_to_h(m, wait_grp(gb), False)
                vec.wait_ge(y0_ready, c.want(y0_ready))
                g = grp()
                vec.tensor_tensor(banks(Y[:]), banks(Y[:]), group(g), ALU.add).then_inc(vec_steps, c.adds(vec_steps))
                vec.wait_ge(vec_steps, c.given(vec_steps))
                vec.sem_inc(grp_free[g], 1)
                for d in range(2):
                    vec.wait_ge(eb_ready, c.want(eb_ready))
                    g = grp()
                    vec.tensor_tensor(banks(T2[:]), group(g), banks(EB[d][:]), ALU.mult)\
                        .then_inc(vec_steps, c.adds(vec_steps))
                    vec.wait_ge(vec_steps, c.given(vec_steps))
                    vec.sem_inc(grp_free[g], 1)
                    vec.tensor_tensor(Y[:], Y[:], T2[:], ALU.add).then_inc(vec_steps, c.adds(vec_steps))
                    vec.wait_ge(vec_steps, c.given(vec_steps))
                vec.wait_ge(zt_in, c.want(zt_in, 16))
                vec.tensor_tensor(Y[:], Y[:], ZT[:], ALU.mult).then_inc(y_ready, c.adds(y_ready))
                vec.wait_ge(y_hi, c.want(y_hi))
                vec.scalar_tensor_tensor(Ylo[:, j % 2, :], Y[:], NORMG[:, j:j + 1],
                                         Yhi[:, j % 2, :].bitcast(F32), ALU.mult, ALU.subtract)\
                    .then_inc(y_split, c.adds(y_split))
                vec.wait_ge(sq_full, c.want(sq_full))
                vec.wait_ge(sq_free, c.given(sq_free))
                vec.tensor_tensor(SS[:], SS[:], SQ[:], ALU.add).then_inc(sq_free, c.adds(sq_free))
            for m in range(KD):
                add_to_h(m, wait_grp(gb), False)
            assert gb[0] == b

        n = TILES_PER_GROUP
        with vec.Fori(0, GROUPS) as i, \
                c.rounds(GROUPS, i,
                         {to_vector[b]: 16, to_vector[b ^ 1]: 21, xtok_ready: n, l_ready: 2 * n, y0_ready: n,
                          eb_ready: 2 * n, zt_in: 16 * n, y_hi: n, sq_full: n},
                         {vec_steps: 37 * n, grp_free[0]: KD, grp_free[1]: KD, xw_ready: 2 * n, y_ready: n,
                          y_split: n, sq_free: n}):
            scan_round(i)
        vec.wait_ge(sq_free, c.given(sq_free))
        vec.sem_inc(sum_ready, 1)
        rms_factor(D_INNER)
        vec.wait_ge(rms_ready, c.want(rms_ready))
        for k in range(KD):
            vec.wait_ge(h_back[k % 2], c.want(h_back[k % 2], 16))
            vec.tensor_tensor(H[:, k, :], H[:, k, :], RMS[:], ALU.mult).then_inc(vec_steps, c.adds(vec_steps))
            vec.wait_ge(vec_steps, c.given(vec_steps))
            vec.tensor_tensor(H[:, k, :], H[:, k, :], M[k % 2][:], ALU.add).then_inc(vec_steps, c.adds(vec_steps))
            vec.wait_ge(vec_steps, c.given(vec_steps))
            vec.sem_inc(h_ready, 1)
            lo_part(k, "ffn1")
        b ^= 1
        b = feed_forward(b, lambda m: add_squares(SS, m == 0, m == KD - 1))
        rms_factor(D_MODEL)
        vec.wait_ge(rms_ready, c.want(rms_ready))
        for k in range(KD):
            vec.scalar_tensor_tensor(H[:, k, :], H[:, k, :], col("final", k), RMS[:], ALU.mult, ALU.mult)\
                .then_inc(out_ready, c.adds(out_ready))

    base.close()


def blocks(w, kt_first=True):
    k, m = w.shape
    return w.reshape(k // P, P, m // P, P).transpose(2, 0, 1, 3)


def pad_to(w, m):
    return np.concatenate([w, np.zeros((w.shape[0], m - w.shape[1]), w.dtype)], 1) if w.shape[1] < m else w


def units(b):
    b = b.reshape(-1, BLK, P, P)
    return b.transpose(0, 2, 1, 3).reshape(len(b), P, BLK * P)


def swapped(rope):
    half = ROPE // 2
    return np.concatenate([rope[..., half:], rope[..., :half]], -1)


def head_order(h, v):
    nope, rope = v[..., :NOPE], v[..., NOPE:]
    parts = (nope, rope, swapped(rope)) if h % 2 == 0 else (rope, swapped(rope), nope)
    return np.concatenate(parts, -1)


def ffn_units(gate, up, down):
    g, u = blocks(gate), blocks(up)
    d = blocks(down)
    steps = []
    for i in range(F_STEPS + 1):
        f = slice(i * F_STEP, (i + 1) * F_STEP)
        cols_ = [x for k in range(*f.indices(F_TILES)) for x in (g[k], u[k])] if i < F_STEPS else []
        prev = d[:, (i - 1) * F_STEP:i * F_STEP].reshape(-1, P, P) if i else None
        if not i:
            steps += cols_
        elif cols_:
            steps += [cols_[0], prev, *cols_[1:]]
        else:
            steps += [prev]
    return np.concatenate(steps)


def weight_stream(a):
    w_in = a["mla_w_in"][0]
    rope = w_in[:, Q_RANK + KV_RANK:]
    rope = np.concatenate([rope, swapped(rope)] * 2, 1)
    parts = [blocks(np.concatenate([w_in[:, :Q_RANK + KV_RANK], rope], 1)).reshape(-1, P, P)]
    q_up = a["mla_w_q_up"][0].reshape(Q_RANK, HEADS, QK)
    kv_up = a["mla_w_kv_up"][0].reshape(KV_RANK, HEADS, NOPE + VD)
    for p in range(PAIRS):
        for h in (2 * p, 2 * p + 1):
            parts.append(head_order(h, q_up[:, h]).reshape(KQ, P, P))
        parts.append(kv_up[:, 2 * p:2 * p + 2, :NOPE].reshape(KKV, P, P))
        parts.append(kv_up[:, 2 * p:2 * p + 2, NOPE:].reshape(KKV, P, P))
        parts.append(np.zeros((BLK - KKV, P, P), w_in.dtype))
    parts.append(blocks(a["mla_w_out"][0]).reshape(-1, P, P))
    parts.append(ffn_units(a["ffn_w_gate"][0], a["ffn_w_up"][0], a["ffn_w_down"][0]))
    if U_DT:
        s_in = a["ssd_w_in"][0]
        z, xbc, dt = np.split(s_in, [D_INNER, D_INNER + CONV_TILES * P], 1)
        parts.append(blocks(pad_to(dt, P)).reshape(-1, P, P))
        parts.append(blocks(xbc).reshape(-1, P, P))
        parts.append(blocks(z).reshape(-1, P, P))
        o = blocks(a["ssd_w_out"][0])
        for j in range(0, Z_TILES, 2):
            parts.append(o[:, j:j + 2].reshape(-1, P, P))
    parts.append(ffn_units(a["ffn_w_gate"][1], a["ffn_w_up"][1], a["ffn_w_down"][1]))
    out = units(np.concatenate(parts))
    assert len(out) == UNITS, (len(out), UNITS)
    return out


def column_table(a):
    def by_tile(v):
        return v.reshape(-1, P).T

    k_head = a["mla_k_head_norm"][0]
    kr = k_head[NOPE:]
    conv = np.concatenate([a["ssd_conv_w"][0], a["ssd_conv_b"]], 0)
    conv = conv.reshape(D_CONV + 1, CONV_TILES, P).transpose(2, 1, 0).reshape(P, -1)
    parts = [by_tile(a["mix_norm"][0]), by_tile(a["ffn_norm"][0]), by_tile(a["mix_norm"][1]),
             by_tile(a["ffn_norm"][1]), by_tile(a["final_norm"]), by_tile(a["mla_q_norm"][0]),
             by_tile(a["mla_kv_norm"][0]),
             np.stack([head_order(h, a["mla_q_head_norm"][0]) for h in range(2)], 1),
             np.concatenate([k_head[:NOPE]] * 2)[:, None],
             np.concatenate([kr, swapped(kr)] * 2)[:, None],
             conv, by_tile(np.repeat(a["ssd_d"][0], SP_)), by_tile(a["ssd_norm"][0])]
    table = np.concatenate(parts, 1)
    assert table.shape == (P, NCOLS)
    return np.ascontiguousarray(table)


def constant_table():
    i = np.arange(P)
    c = np.zeros((P, NCONST), np.float32)
    c[:, C_IDENT:C_IDENT + P] = i[:, None] == i
    c[:, C_PAIR:C_PAIR + P] = (i[:, None] // NOPE == i // NOPE) & (i[:, None] % ROPE == i % ROPE)
    c[:, C_UPPER:C_UPPER + P] = i[:, None] <= i
    c[:, C_LOWER:C_LOWER + P] = i[:, None] >= i
    c[:, C_ONES:C_ONES + P] = 1
    c[:, C_STRICT_LOWER:C_STRICT_LOWER + P] = i[:, None] > i
    c[:, C_STRICT_UPPER:C_STRICT_UPPER + P] = i[:, None] < i
    for m, marked in ((M_QE, i < QK), (M_QO, (i < ROPE) | (i >= NOPE)), (M_KE, i < NOPE), (M_KO, i >= NOPE),
                      (M_ROPE, i < ROPE)):
        c[:, C_MASK + m] = marked
    return c


def rotation_tables():
    half = ROPE // 2
    inv_freq = (10000.0 ** (-np.arange(half, dtype=np.float32) / half)).astype(np.float32)
    ang = np.arange(L, dtype=np.float32)[:, None] * inv_freq[None, :]
    cos, sin = np.cos(ang).T, np.sin(ang).T
    turn = np.concatenate([cos, cos, -sin, sin], 0)
    plain = np.ones((NOPE, L), np.float32)
    return np.stack([np.concatenate(x, 0) for x in ((plain, turn), (turn, plain), (turn, turn))]).astype(np.float32)


def kernel(**inputs):
    import concourse.bacc as bacc
    from concourse.bass_utils import run_bass_kernel_spmd

    a = {k: np.asarray(v) for k, v in inputs.items()}
    seqs_ = [np.concatenate([a["meta_tokens"], a[x][0]], 0) for x in ("x_prompt", "x_sample")]
    rows = np.stack([a["ssd_dt_bias"][0].reshape(-1), a["ssd_a_log"][0].reshape(-1)])
    arrays = {
        "x": np.ascontiguousarray(np.concatenate(seqs_, 0).T.reshape(KD, P, T)),
        "w": weight_stream(a),
        "cols": column_table(a),
        "rows": np.ascontiguousarray(np.broadcast_to(rows[None], (CH, 2, 2 * SHEADS))),
        "const": constant_table(),
        "trig": rotation_tables(),
    }
    nc = bacc.Bacc("TRN2", target_bir_lowering=False, num_devices=1)
    tensors = {n: nc.dram_tensor("in_" + n, v.shape, mybir.dt.from_np(v.dtype), kind="ExternalInput").ap()
               for n, v in arrays.items()}
    tensors["out"] = nc.dram_tensor("out", (KD, P, T), F32, kind="ExternalOutput").ap()
    encoder(nc, tensors)
    r = run_bass_kernel_spmd(nc, [{"in_" + n: v for n, v in arrays.items()}], core_ids=[0])
    out = np.asarray(r.results[0]["out"]).reshape(D_MODEL, NSEQ, L)
    return tuple(np.ascontiguousarray(out[:, s, N_META:].T)[None] for s in range(NSEQ))
```

```python
import math
from contextlib import ExitStack, contextmanager

import numpy as np

import concourse.bass as bass
from concourse import mybir

F32 = mybir.dt.float32
F32R = mybir.dt.float32r
I32 = mybir.dt.int32
ALU = mybir.AluOpType
ACT = mybir.ActivationFunctionType
AX_X = mybir.AxisListType.X
AX_XY = mybir.AxisListType.XY

P = 128
D_MODEL = 1024
N_META = 16
SEQ = 512
NSEQ = 2
L = N_META + SEQ
T = NSEQ * L
CH = 88
NC = T // CH
CS = L // CH
NB = 3
NT = T // NB
CB = NC // NB
KD = D_MODEL // P
EPS = 1e-6

HEADS, NOPE, ROPE, VD = 16, 64, 32, 64
QK = NOPE + ROPE
PAIRS = HEADS // 2
Q_RANK, KV_RANK = 384, 256
KQ, KKV = Q_RANK // P, KV_RANK // P

D_INNER, GROUPS, D_STATE, D_CONV, SHEADS, SP_ = 2048, 4, 128, 5, 32, 64
CONV_TILES = (D_INNER + 2 * GROUPS * D_STATE) // P
Z_TILES = D_INNER // P
TILES_PER_GROUP = Z_TILES // GROUPS
HPG = SHEADS // GROUPS

FFN = 2816
F_TILES = FFN // P
F_STEP = 2
F_STEPS = F_TILES // F_STEP

BLK = 8

U_MLA_IN = KQ + KKV + 1
U_PAIR = 2
U_OUT = KD
U_FFN = F_TILES * 3
U_DT = 1
U_SSD_IN = CONV_TILES + Z_TILES
U_SSD_OUT = Z_TILES * KD // BLK
U0_PAIR = U_MLA_IN
U0_OUT = U0_PAIR + PAIRS * U_PAIR
U0_FFN0 = U0_OUT + U_OUT
U0_DT = U0_FFN0 + U_FFN
U0_SSD_IN = U0_DT + U_DT
U0_SSD_OUT = U0_SSD_IN + U_SSD_IN
U0_FFN1 = U0_SSD_OUT + U_SSD_OUT
UNITS = U0_FFN1 + U_FFN

COLS = {}
_n = 0
for _name, _w in (("mix0", KD), ("ffn0", KD), ("mix1", KD), ("ffn1", KD), ("final", KD),
                  ("q_norm", KQ), ("kv_norm", KKV), ("q_head", 2), ("k_nope", 1), ("k_rope", 1),
                  ("conv", CONV_TILES * (D_CONV + 1)), ("skip", Z_TILES), ("ssd_norm", Z_TILES)):
    COLS[_name] = _n
    _n += _w
NCOLS = _n

C_IDENT, C_PAIR, C_UPPER, C_LOWER, C_ONES, C_STRICT_LOWER, C_STRICT_UPPER, C_MASK = (P * k for k in range(8))

B_SCAN, B_FFN1, B_LAST = 1, 1, 1
M_QE, M_QO, M_KE, M_KO, M_ROPE = range(5)
NCONST = C_MASK + 5

S_R1, S_R1SQ, S_A, S_B, S_A2, S_B2, S_RR, S_V, S_TMP, S_QS, S_KF = 0, 1, 2, 3, 4, 5, 6, 7, 9, 11, 13

INPUTS = ("x", "w", "cols", "rows", "const", "trig")


class Counts:

    def __init__(self):
        self.seen, self.made, self.running = {}, {}, []

    def _value(self, which, sem):
        n = (self.seen, self.made)[which].get(sem.name, 0)
        for i, per in self.running:
            if per[which].get(sem.name, 0):
                n = i * per[which][sem.name] + n
        return n

    def want(self, sem, k=1):
        self.seen[sem.name] = self.seen.get(sem.name, 0) + k
        return self._value(0, sem)

    def ahead(self, sem, k=1):
        return self._value(0, sem) + k

    def adds(self, sem, k=1):
        self.made[sem.name] = self.made.get(sem.name, 0) + k
        return k

    def given(self, sem):
        assert self.made.get(sem.name, 0) > 0
        return self._value(1, sem)

    @contextmanager
    def rounds(self, trips, i, seen, made):
        per = ({s.name: k for s, k in seen.items()}, {s.name: k for s, k in made.items()})
        start = (dict(self.seen), dict(self.made))
        self.running.append((i, per))
        yield
        self.running.pop()
        for which, counts in enumerate((self.seen, self.made)):
            found = {s: n - start[which].get(s, 0) for s, n in counts.items() if n != start[which].get(s, 0)}
            if found != {s: k for s, k in per[which].items() if k}:
                raise ValueError(f"{('seen', 'made')[which]} per round: {found}")
            for s, k in found.items():
                counts[s] = start[which].get(s, 0) + trips * k


def chunks(ap):
    return ap.rearrange("p (c t) -> p c t", t=CH)


def banks(ap):
    return ap.rearrange("p (b n) -> p b n", b=NB)


def seqs(ap):
    return ap.rearrange("p (s n) -> p s n", s=NSEQ)


def encoder(nc, tensors):
    base = ExitStack()

    def sem(name):
        return base.enter_context(nc.semaphore(name))

    def sb(name, shape, dt=F32, stack=None):
        return (stack or base).enter_context(nc.sbuf_tensor(name, shape, dt))

    x_d, w_d, cols_d, rows_d, const_d, trig_d, out_d = (tensors[n] for n in INPUTS + ("out",))
    scratch_d = nc.dram_tensor("scratch", (CONV_TILES + Z_TILES + KD, P, T), F32, kind="Internal").ap()
    D_Z, D_H = CONV_TILES, CONV_TILES + Z_TILES

    Wraw = [sb(f"Wraw{s}", [P, BLK, P]) for s in range(2)]
    Whi = [sb(f"Whi{s}", [P, BLK, P], F32R) for s in range(2)]
    Wlo = [sb(f"Wlo{s}", [P, BLK, P], F32R) for s in range(2)]
    H = sb("H", [P, KD, T])
    cols = sb("cols", [P, NCOLS])
    const = sb("const", [P, NCONST])
    STAT = sb("STAT", [CH, 26, NC])
    SQ = sb("SQ", [P, T])
    SS = sb("SS", [P, T])
    RMS = sb("RMS", [P, T])

    KS = sb("KS", [CH, NC, 4])
    SMAX, SSUM, SINV = (sb(n, [CH, 2 * NC]) for n in ("SMAX", "SSUM", "SINV"))

    ident = const[:, C_IDENT:C_IDENT + P]
    ident_ch = const[0:CH, C_IDENT:C_IDENT + CH]
    pair_sum = const[:, C_PAIR:C_PAIR + P]
    upper = const[0:CH, C_UPPER:C_UPPER + CH]
    lower = const[0:CH, C_LOWER:C_LOWER + CH]
    strict_lower = const[0:CH, C_STRICT_LOWER:C_STRICT_LOWER + CH]
    strict_upper = const[0:CH, C_STRICT_UPPER:C_STRICT_UPPER + CH]
    one = const[:, C_ONES:C_ONES + 1]
    ones = const[:, C_ONES:C_ONES + P]
    ones_ch = const[0:CH, C_ONES:C_ONES + P]

    def mask(k, n=1):
        return const[:, C_MASK + k:C_MASK + k + n]

    def col(name, k=0, n=1):
        return cols[:, COLS[name] + k:COLS[name] + k + n]

    def stat(k, n=1):
        return STAT[:, k, :] if n == 1 else STAT[:, k:k + n, :]

    low = ExitStack()
    Uhi, Ulo = sb("Uhi", [P, KD, T], F32R, low), sb("Ulo", [P, KD, T], F32R, low)
    with ExitStack() as s:
        Chi, Clo = sb("Chi", [P, KQ + KKV, T], F32R, s), sb("Clo", [P, KQ + KKV, T], F32R, s)
        KR = [sb(f"KR{h}", [P, T], F32, s) for h in range(2)]
        SSQ = [sb(f"SSQ{k}", [P, T], F32, s) for k in range(2)]
        CF = [sb(f"CF{k}", [P, T], F32, s) for k in range(2)]
    trig_k = RMS[:, 0:L]
    with ExitStack() as s:
        Ohi, Olo = sb("Ohi", [P, KD, T], F32R, s), sb("Olo", [P, KD, T], F32R, s)
    with ExitStack() as s:
        GATE, SILU, HID = (sb(n, [P, T], F32, s) for n in ("GATE", "SILU", "HID"))
        HIDhi, HIDlo = sb("HIDhi", [P, F_STEP, T], F32R, s), sb("HIDlo", [P, F_STEP, T], F32R, s)
    with ExitStack() as s:
        DT, A, WST = (sb(n, [CH, 2, NC, SHEADS], F32, s) for n in ("DT", "A", "WST"))
        DECAY = sb("DECAY", [P, 2, NC, SHEADS], F32, s)
        with ExitStack() as s2:
            XC = sb("XC", [P, T], F32, s2)
            YC = [sb(f"YC{k}", [P, T], F32, s2) for k in range(2)]
            E1, E2, E3, CSUM = (sb(n, [CH, 2, NC, SHEADS], F32, s2) for n in ("E1", "E2", "E3", "CSUM"))
            ROWS = sb("ROWS", [CH, 2, 2, SHEADS], F32, s2)
            TAPS = sb("TAPS", [P, D_CONV + 1], F32, s2)
        with ExitStack() as s2:
            M = [sb(f"M{h}", [P, T], F32, s2) for h in range(2)]
            XW = [sb(f"XW{d}", [CH, NC, P], F32, s2) for d in range(2)]
            ST = sb("ST", [P, 2, NC, P], F32, s2)
            EB0 = sb("EB0", [P, T], F32, s2)
            STEP = sb("STEP", [CH, 2 * CH + P], F32R, s2)
            Yhi, Ylo = sb("Yhi", [P, 2, T], F32R, s2), sb("Ylo", [P, 2, T], F32R, s2)
    low.close()
    with ExitStack() as s:
        Q = [sb(f"Q{h}", [P, T], F32, s) for h in range(2)]
        QR = [sb(f"QR{h}", [P, T], F32, s) for h in range(2)]
        SQH = [sb(f"SQH{h}", [P, T], F32, s) for h in range(3)]
        KM = [sb(f"KM{h}", [P, T], F32, s) for h in range(2)]
        V = sb("V", [CH, NC, P], F32, s)
        PR = [sb(f"PR{h}", [CH, L], F32, s) for h in range(2)]
        PT = [sb(f"PT{h}", [CH, CS, CH], F32, s) for h in range(2)]
        O = sb("O", [CH, NC, P], F32, s)
        trig_q = sb("trig_q", [P, 2, L], F32, s)
    with ExitStack() as s:
        BT, CT, XT, ZT, Y = (sb(n, [P, T], F32, s) for n in ("BT", "CT", "XT", "ZT", "Y"))
        BTOK, XTOK = sb("BTOK", [CH, NC, P], F32, s), sb("XTOK", [CH, NC, P], F32, s)
        G = [sb(f"G{d}", [CH, NC, CH], F32, s) for d in range(2)]
        VHI = [sb(f"VHI{d}", [CH, NC, CH], F32R, s) for d in range(2)]
        VLO = [sb(f"VLO{d}", [CH, NC, CH], F32R, s) for d in range(2)]
        T2 = sb("T2", [P, T], F32, s)
        DTG, WG = (sb(n, [CH, 2, NC, HPG], F32, s) for n in ("DTG", "WG"))
        AHI, ALO = (sb(n, [CH, 2, NC, HPG], F32R, s) for n in ("AHI", "ALO"))
        DECG = sb("DECG", [P, 2, NC, HPG], F32, s)
        SKIPG, NORMG = (sb(n, [P, TILES_PER_GROUP], F32, s) for n in ("SKIPG", "NORMG"))

    EB = [EB0, RMS]
    TM = chunks(BT[0:CH, :])
    STEPS = (STEP[:, 0:CH], STEP[:, CH:2 * CH])
    ONES = STEP[:, 2 * CH:2 * CH + P]

    PS = base.enter_context(nc.psum_tensor("PS", [P, 8, 512], F32))
    STAT_BANK = 6

    def group(b, n=NT, parts=P, at=0):
        return PS[at:at + parts, NB * b:NB * b + NB, 0:n]

    def piece(b, c, width, parts=CH, at=0):
        k = c % CB * width
        return PS[at:at + parts, NB * b + c // CB, k:k + width]

    raw_full = [sem(f"raw_full{s}") for s in range(2)]
    w_full = [sem(f"w_full{s}") for s in range(2)]
    w_free = [sem(f"w_free{s}") for s in range(2)]
    to_vector = [sem(f"to_vector{b}") for b in range(2)]
    to_scalar = [sem(f"to_scalar{b}") for b in range(2)]
    grp_free = [sem(f"grp_free{b}") for b in range(2)]
    vec_steps, act_steps, pool_steps = sem("vec_steps"), sem("act_steps"), sem("pool_steps")
    const_in = sem("const_in")
    x_in = [sem(f"x_in{k}") for k in range(KD)]
    h_ready = sem("h_ready")
    hi_ready, u_ready = sem("hi_ready"), sem("u_ready")
    sq_full, sq_free, sum_ready = sem("sq_full"), sem("sq_free"), sem("sum_ready")
    stat_full, row_ready = sem("stat_full"), sem("row_ready")
    scan_free = sem("scan_free")
    rms_ready = sem("rms_ready")
    trig_in, rope_sq, rope_ready = sem("trig_in"), sem("rope_sq"), sem("rope_ready")
    q_squared, k_squared = sem("q_squared"), sem("k_squared")
    q_ready, ks_ready = sem("q_ready"), sem("ks_ready")
    km_ready, v_ready = sem("km_ready"), sem("v_ready")
    sc_full, nb_ready, p_full = sem("sc_full"), sem("nb_ready"), sem("p_full")
    pt_full, pt_ready, rinv_ready = sem("pt_full"), sem("pt_ready"), sem("rinv_ready")
    ov_full, ov_free, o_ready = sem("ov_full"), sem("ov_free"), sem("o_ready")
    o_split, h_loaded = sem("o_split"), sem("h_loaded")
    gate_ready, silu_ready, hid_ready = sem("gate_ready"), sem("silu_ready"), sem("hid_ready")
    hid_hi, hid_split = sem("hid_hi"), sem("hid_split")
    out_ready, out_done = sem("out_ready"), sem("out_done")
    yc_ready, yc_out = sem("yc_ready"), [sem(f"yc_out{k}") for k in range(2)]
    rows_in, h_saved, h_cleared, dt_raw = (sem(n) for n in ("rows_in", "h_saved", "h_cleared", "dt_raw"))
    exp_in, exp_out, a_ready = sem("exp_in"), sem("exp_out"), sem("a_ready")
    staged, v_full = sem("staged"), sem("v_full")
    v_used = [sem(f"v_used{d}") for d in range(2)]
    st_in, eb_free = sem("st_in"), sem("eb_free")
    xw1_ready, y_squared, ss_added = sem("xw1_ready"), sem("y_squared"), sem("ss_added")
    bt_in, ct_in, xt_in, zt_in = sem("bt_in"), sem("ct_in"), sem("xt_in"), sem("zt_in")
    btok_ready, g_ready = sem("btok_ready"), sem("g_ready")
    xtok_ready, y0_ready, l_ready, m_ready = (sem(n) for n in ("xtok_ready", "y0_ready", "l_ready", "m_ready"))
    eb_ready, xw_ready, st_ready = sem("eb_ready"), sem("xw_ready"), sem("st_ready")
    y_ready, y_hi, y_split, h_back = sem("y_ready"), sem("y_hi"), sem("y_split"), [sem(f"h_back{k}") for k in range(2)]

    block = base.enter_context(nc.Block())

    def dcol(tensor, d, h):
        return tensor[:, d, :, h]

    @block.sync
    def _(sp):
        c = Counts()

        def load(u, s):
            sp.dma_start(Wraw[s][:], w_d[u].rearrange("p (k m) -> p k m", m=P)
                         if isinstance(u, int) else
                         w_d[bass.ds(u, 1)].rearrange("o p (k m) -> p (o k) m", m=P)).then_inc(raw_full[s], 16)

        for u in range(2):
            load(u, u)
        pairs = (UNITS - 2) // 2
        with sp.Fori(0, pairs) as i, \
                c.rounds(pairs, i,
                         {w_full[0]: 1, w_full[1]: 1},
                         {}):
            for s in range(2):
                sp.wait_ge(w_full[s], c.want(w_full[s]))
                load(i * 2 + (2 + s), s)
        for u in range(2 + 2 * pairs, UNITS):
            sp.wait_ge(w_full[u % 2], c.want(w_full[u % 2]))
            load(u, u % 2)

    @block.gpsimd
    def _(pool):
        c = Counts()

        def split(s):
            pool.wait_ge(raw_full[s], c.want(raw_full[s], 16))
            pool.wait_ge(w_free[s], c.want(w_free[s]))
            pool.tensor_tensor(Whi[s][:], Wraw[s][:], ones.unsqueeze(1).broadcast_to([P, BLK, P]), ALU.mult)\
                .then_inc(pool_steps, c.adds(pool_steps))
            pool.wait_ge(pool_steps, c.given(pool_steps))
            pool.tensor_tensor(Wlo[s][:], Wraw[s][:], Whi[s][:].bitcast(F32), ALU.subtract)\
                .then_inc(w_full[s], c.adds(w_full[s]))

        def split_units(u0, n):
            per = {pool_steps: 2, w_full[0]: 1, w_full[1]: 1}
            with pool.Fori(0, n // 2) as i, \
                    c.rounds(n // 2, i,
                             {raw_full[0]: 16, raw_full[1]: 16, w_free[0]: 1, w_free[1]: 1},
                             per):
                for k in range(2):
                    split((u0 + k) % 2)
            if n % 2:
                split((u0 + n - 1) % 2)

        pool.wait_ge(const_in, c.want(const_in, 16 * 2))
        split_units(0, U0_SSD_OUT)
        pool.wait_ge(h_saved, c.want(h_saved, 16 * KD))
        pool.memset(H[:], 0.0).then_inc(h_cleared, c.adds(h_cleared))

        def build_v(h):
            for d, m in ((0, upper), (1, lower)):
                pool.wait_ge(v_used[d], c.want(v_used[d]))
                for part, of in ((VHI, AHI), (VLO, ALO)):
                    ins = pool.tensor_tensor(part[d][:], m.unsqueeze(1).broadcast_to([CH, NC, CH]),
                                             dcol(of, d, h).unsqueeze(2).broadcast_to([CH, NC, CH]), ALU.mult)
                    if of is AHI:
                        ins.then_inc(pool_steps, c.adds(pool_steps))
                ins.then_inc(v_full, c.adds(v_full))

        def weigh_x():
            pool.wait_ge(xtok_ready, c.want(xtok_ready))
            pool.tensor_tensor(XW[1][:].rearrange("p c (e n) -> p c e n", e=2),
                               XTOK[:].rearrange("p c (e n) -> p c e n", e=2),
                               WG[:, 1, :, h:h + 2].unsqueeze(3).broadcast_to([CH, NC, 2, SP_]),
                               ALU.mult).then_inc(xw1_ready, c.adds(xw1_ready))

        def add_output_squares():
            pool.wait_ge(y_squared, c.want(y_squared))
            pool.tensor_tensor(SS[:], SS[:], SQ[:], ALU.add).then_inc(pool_steps, c.adds(pool_steps))
            pool.wait_ge(pool_steps, c.given(pool_steps))
            pool.sem_inc(ss_added, 1)

        with pool.Fori(0, GROUPS) as i, \
                c.rounds(GROUPS, i,
                         {staged: 1, xtok_ready: TILES_PER_GROUP, y_squared: TILES_PER_GROUP, v_used[0]: HPG, v_used[1]: HPG,
                          raw_full[0]: 32, raw_full[1]: 32, w_free[0]: 2, w_free[1]: 2},
                         {pool_steps: 2 * HPG + 8, v_full: 2 * HPG, w_full[0]: 2, w_full[1]: 2,
                          xw1_ready: TILES_PER_GROUP}):
            pool.wait_ge(staged, c.want(staged))
            for j in range(TILES_PER_GROUP):
                h = 2 * j
                build_v(h)
                weigh_x()
                if j == 2:
                    split((U0_SSD_OUT + 1) % 2)
                build_v(h + 1)
                if j:
                    add_output_squares()
                if j != 1:
                    split((U0_SSD_OUT + j) % 2)
            add_output_squares()
        pool.sem_inc(sum_ready, 1)
        split_units(U0_FFN1, U_FFN)

    @block.tensor
    def _(pe):
        c = Counts()
        now = {"slot": None, "release": None}

        def mm(out, lhsT, rhs, start=True, stop=True):
            ins = pe.matmul(out, lhsT, rhs, start=start, stop=stop, skip_group_check=True)
            if now["release"] is not None:
                ins.then_inc(w_free[now["release"]], c.adds(w_free[now["release"]]))
                now["release"] = None
            return ins

        def enter_unit(u):
            s = u % 2
            pe.wait_ge(w_full[s], c.want(w_full[s]))
            now["release"], now["slot"] = now["slot"], s

        def product(out, blocks, Xhi, Xlo, kts, ready=None, n0=0, k_total=None):
            last = (k_total or len(kts)) - 1
            for j, (blk, kt) in enumerate(zip(blocks, kts)):
                if ready is not None:
                    pe.wait_ge(ready, c.want(ready))
                for p, (W, X) in enumerate(((Whi, Xhi), (Whi, Xlo), (Wlo, Xhi))):
                    for n in range(NB):
                        ins = mm(out[:, n, :], W[now["slot"]][:, blk, :], X[:, kt, n * NT:(n + 1) * NT],
                                 start=(j == 0 and p == 0), stop=(j == last and p == 2))
            return ins

        def sums_by_token(k, src, rhs):
            n = rhs.shape[1]
            for ch in range(NC):
                ins = mm(PS[0:CH, STAT_BANK, k * NC:(k + n) * NC].rearrange("p (k c) -> p k c", c=NC)[:, :, ch],
                         src[:, ch * CH:(ch + 1) * CH], rhs)
            return ins

        def spread_rms(b):
            pe.wait_ge(row_ready, c.want(row_ready))
            pe.wait_ge(grp_free[b], c.want(grp_free[b]))
            for ch in range(NC):
                ins = mm(piece(b, ch, CH, P), STAT[:, S_R1, ch:ch + 1].broadcast_to([CH, P]), ident_ch)
            ins.then_inc(to_scalar[b], c.adds(to_scalar[b]))

        pe.wait_ge(const_in, c.want(const_in, 16 * 2))
        for m in range(U_MLA_IN):
            enter_unit(m)
            pe.wait_ge(grp_free[m % 2], c.want(grp_free[m % 2]))
            product(group(m % 2), range(KD), Uhi, Ulo, range(KD), u_ready if m == 0 else None)\
                .then_inc(to_scalar[m % 2], c.adds(to_scalar[m % 2]))
        pe.wait_ge(sum_ready, c.want(sum_ready))
        sums_by_token(0, SS, one)
        pe.wait_ge(sum_ready, c.want(sum_ready))
        sums_by_token(1, SSQ[0], one)
        pe.wait_ge(sum_ready, c.want(sum_ready))
        sums_by_token(2, SSQ[1], one)
        pe.wait_ge(rope_sq, c.want(rope_sq))
        sums_by_token(3, SQ, mask(M_ROPE)).then_inc(stat_full, c.adds(stat_full))
        pe.wait_ge(rope_ready, c.want(rope_ready))
        pe.wait_ge(grp_free[0], c.want(grp_free[0]))
        for n in range(NB):
            ins = mm(group(0)[:, n, :], pair_sum, CF[0][:, n * NT:(n + 1) * NT])
        ins.then_inc(to_scalar[0], c.adds(to_scalar[0]))
        pe.wait_ge(u_ready, c.want(u_ready, KQ + KKV))
        pe.wait_ge(row_ready, c.want(row_ready))

        steps = [(h, s, t) for h in range(2) for s in range(NSEQ) for t in range(CS)]
        NS = len(steps)

        def attention_round():
            enter_unit(U0_PAIR)
            for n, h in enumerate((2, 0, 1)):
                b = n % 2
                pe.wait_ge(grp_free[b], c.want(grp_free[b]))
                if h < 2:
                    ins = product(group(b), range(KQ * h, KQ * h + KQ), Chi, Clo, range(KQ))
                else:
                    ins = product(group(b), range(2 * KQ, 2 * KQ + KKV), Chi, Clo, range(KQ, KQ + KKV))
                ins.then_inc(to_scalar[b], c.adds(to_scalar[b]))
                if h == 0:
                    pe.wait_ge(k_squared, c.want(k_squared))
                    sums_by_token(2, SQH[2], mask(M_KE, 2)).then_inc(stat_full, c.adds(stat_full))
            enter_unit(U0_PAIR + 1)
            pe.wait_ge(grp_free[1], c.want(grp_free[1]))
            for ch in range(NC):
                t = slice(ch * CH, (ch + 1) * CH)
                for k in range(KKV):
                    for p, (X, W) in enumerate(((Chi, Whi), (Clo, Whi), (Chi, Wlo))):
                        ins = mm(piece(1, ch, P), X[:, KQ + k, t], W[now["slot"]][:, k, :],
                                 start=(k == 0 and p == 0), stop=(k == KKV - 1 and p == 2))
            ins.then_inc(to_vector[1], c.adds(to_vector[1]))
            pe.wait_ge(ks_ready, c.want(ks_ready))
            for h in range(2):
                pe.wait_ge(grp_free[h], c.want(grp_free[h]))
                for ch in range(NC):
                    for part in range(2):
                        ins = mm(piece(h, ch, CH, NOPE, part * NOPE),
                                 KS[:, ch, 2 * h + part:2 * h + part + 1].broadcast_to([CH, NOPE]), ident_ch)
                ins.then_inc(to_vector[h], c.adds(to_vector[h]))
            for h in range(2):
                pe.wait_ge(q_squared, c.want(q_squared))
                ins = sums_by_token(h, SQH[h], mask((M_QE, M_QO)[h]))
            ins.then_inc(stat_full, c.adds(stat_full))
            pe.wait_ge(q_ready, c.want(q_ready, 2))
            pe.wait_ge(v_ready, c.want(v_ready))
            pe.wait_ge(grp_free[0], c.ahead(grp_free[0]))
            pe.wait_ge(grp_free[1], c.ahead(grp_free[1]))
            pe.wait_ge(km_ready, c.want(km_ready, 2))
            for n in range(NS + 2):
                if n < NS:
                    h, s, t = steps[n]
                    at = (s * CS + t) * CH
                    for j in range(2):
                        ins = mm(PS[0:CH, 2 * (n % 2) + j, 0:L // 2], Q[h][:, at:at + CH],
                                 KM[h][:, s * L + j * (L // 2):s * L + (j + 1) * (L // 2)])
                    ins.then_inc(sc_full, c.adds(sc_full))
                if n >= 2:
                    pe.wait_ge(pt_ready, c.want(pt_ready))
                if 1 <= n <= NS:
                    pe.wait_ge(p_full, c.want(p_full))
                    for j in range(CS):
                        ins = pe.transpose(PS[0:CH, 4 + j // 3, j % 3 * CH:(j % 3 + 1) * CH],
                                           PR[(n - 1) % 2][:, j * CH:(j + 1) * CH], ident_ch)
                    ins.then_inc(pt_full, c.adds(pt_full))
                if n >= 2:
                    h, s, t = steps[n - 2]
                    pe.wait_ge(ov_free, c.want(ov_free))
                    for j in range(CS):
                        ins = mm(PS[0:CH, 6 + n % 2, 0:VD], PT[n % 2][:, j, :],
                                 V[:, s * CS + j, h * VD:(h + 1) * VD], start=(j == 0), stop=(j == CS - 1))
                    ins.then_inc(ov_full, c.adds(ov_full))
            pe.wait_ge(ov_free, c.ahead(ov_free, 2))
            pe.wait_ge(grp_free[0], c.want(grp_free[0]))
            for ch in range(NC):
                ins = pe.transpose(piece(0, ch, CH, P), O[:, ch, :], ident_ch)
            ins.then_inc(to_scalar[0], c.adds(to_scalar[0]))

        with pe.Fori(0, PAIRS) as i, \
                c.rounds(PAIRS, i,
                         {w_full[0]: 1, w_full[1]: 1, grp_free[0]: 4, grp_free[1]: 3, q_squared: 2,
                          k_squared: 1, ks_ready: 1, q_ready: 2, v_ready: 1, km_ready: 2, pt_ready: NS,
                          p_full: NS, ov_free: NS},
                         {w_free[0]: 1, w_free[1]: 1, to_scalar[0]: 3, to_scalar[1]: 1, to_vector[0]: 1,
                          to_vector[1]: 2, stat_full: 2, sc_full: NS, pt_full: NS, ov_full: NS}):
            attention_round()

        for m in range(U_OUT):
            enter_unit(U0_OUT + m)
            pe.wait_ge(grp_free[m % 2], c.want(grp_free[m % 2]))
            product(group(m % 2), range(KD), Ohi, Olo, range(KD), o_split if m == 0 else None)\
                .then_inc(to_vector[m % 2], c.adds(to_vector[m % 2]))

        def feed_forward(u0, b0):
            b = [b0]

            def grp():
                b[0] ^= 1
                return b[0] ^ 1

            def column(u, ready=None):
                g = grp()
                enter_unit(u)
                pe.wait_ge(grp_free[g], c.want(grp_free[g]))
                product(group(g), range(KD), Uhi, Ulo, range(KD), ready).then_inc(to_vector[g], c.adds(to_vector[g]))

            def down(u):
                pe.wait_ge(hid_split, c.want(hid_split, F_STEP))
                for m in range(KD):
                    if m % (BLK // F_STEP) == 0:
                        enter_unit(u + m // (BLK // F_STEP))
                    g = grp()
                    pe.wait_ge(grp_free[g], c.want(grp_free[g]))
                    product(group(g), [m * F_STEP % BLK + k for k in range(F_STEP)],
                            HIDhi, HIDlo, range(F_STEP)).then_inc(to_vector[g], c.adds(to_vector[g]))

            column(u0, u_ready)
            pe.wait_ge(sum_ready, c.want(sum_ready))
            sums_by_token(0, SS, one).then_inc(stat_full, c.adds(stat_full))
            spread_rms(grp())
            for k in range(1, 2 * F_STEP):
                column(u0 + k)
            per = 2 * F_STEP + 2
            with pe.Fori(0, F_STEPS - 1) as i, \
                    c.rounds(F_STEPS - 1, i,
                             {w_full[0]: 3, w_full[1]: 3, grp_free[0]: 6, grp_free[1]: 6, hid_split: F_STEP},
                             {w_free[0]: 3, w_free[1]: 3, to_vector[0]: 6, to_vector[1]: 6}):
                column(u0 + 2 * F_STEP)
                down(u0 + 2 * F_STEP + 1)
                for k in range(1, 2 * F_STEP):
                    column(u0 + 2 * F_STEP + 2 + k)
            down(u0 + 2 * F_STEP + per * (F_STEPS - 1))
            return b[0]

        b = feed_forward(U0_FFN0, 0)

        def other(b):
            return b ^ 1

        enter_unit(U0_DT)
        pe.wait_ge(grp_free[b], c.want(grp_free[b]))
        product(group(b), range(KD), Uhi, Ulo, range(KD), u_ready).then_inc(to_scalar[b], c.adds(to_scalar[b]))
        pe.wait_ge(sum_ready, c.want(sum_ready))
        sums_by_token(0, SS, one).then_inc(stat_full, c.adds(stat_full))
        pe.wait_ge(dt_raw, c.want(dt_raw))
        pe.wait_ge(grp_free[b], c.want(grp_free[b]))
        for ch in range(NC):
            ins = pe.transpose(piece(b, ch, 2 * SHEADS), XC[0:2 * SHEADS, ch * CH:(ch + 1) * CH],
                               ident[0:2 * SHEADS, 0:2 * SHEADS])
        ins.then_inc(to_vector[b], c.adds(to_vector[b]))
        spread_rms(other(b))
        for u0, n in ((U0_SSD_IN, CONV_TILES), (U0_SSD_IN + CONV_TILES, Z_TILES)):
            with pe.Fori(0, n // 2) as i, \
                    c.rounds(n // 2, i,
                             {w_full[0]: 1, w_full[1]: 1, grp_free[0]: 1, grp_free[1]: 1},
                             {w_free[0]: 1, w_free[1]: 1, to_vector[0]: 1, to_vector[1]: 1}):
                for k, g in ((0, b), (1, other(b))):
                    enter_unit(u0 + k)
                    pe.wait_ge(grp_free[g], c.want(grp_free[g]))
                    product(group(g), range(KD), Uhi, Ulo, range(KD)).then_inc(to_vector[g], c.adds(to_vector[g]))
        pe.wait_ge(a_ready, c.want(a_ready))
        for g, by in ((b, (upper, lower)), (other(b), (ones_ch, ones_ch))):
            pe.wait_ge(grp_free[g], c.want(grp_free[g]))
            for d in range(2):
                ins = mm(PS[0:by[d].shape[1], NB * g + d, 0:NC * SHEADS], by[d],
                         A[:, d].rearrange("p c h -> p (c h)"))
            ins.then_inc(to_vector[g], c.adds(to_vector[g]))

        def scan_round():
            gb = [b]

            def grp():
                gb[0] ^= 1
                pe.wait_ge(grp_free[gb[0] ^ 1], c.want(grp_free[gb[0] ^ 1]))
                return gb[0] ^ 1

            def chunk(ap, ch):
                return ap[:, ch * CH:(ch + 1) * CH]

            def transposes(src):
                g = grp()
                for ch in range(NC):
                    ins = pe.transpose(piece(g, ch, P), chunk(src, ch), ident)
                ins.then_inc(to_scalar[g], c.adds(to_scalar[g]))

            def products_with_v(d, lhsT, g, start, stop):
                for n in range(NB):
                    for part in (VHI, VLO):
                        ins = mm(PS[0:lhsT.shape[1], NB * g + n, 0:NT], lhsT,
                                 part[d][:].rearrange("p c t -> p (c t)")[:, n * NT:(n + 1) * NT],
                                 start=start and part is VHI, stop=stop and part is VLO)
                return ins

            def head():
                pe.wait_ge(v_full, c.want(v_full))
                g = grp()
                products_with_v(0, ONES, g, True, True).then_inc(to_scalar[g], c.adds(to_scalar[g]))
                g = grp()
                products_with_v(0, STEPS[0], g, True, False).then_inc(v_used[0], c.adds(v_used[0]))
                pe.wait_ge(v_full, c.want(v_full))
                products_with_v(1, STEPS[1], g, False, True).then_inc(to_scalar[g], c.adds(to_scalar[g]))
                g = grp()
                products_with_v(1, ONES, g, True, True).then_inc(to_scalar[g], c.adds(to_scalar[g]))

            def out_projection(u):
                enter_unit(u)
                for m in range(KD // 2):
                    g = grp()
                    product(group(g), [m * 2 + k for k in range(2)], Yhi, Ylo, range(2))\
                        .then_inc(to_vector[g], c.adds(to_vector[g]))

            pe.wait_ge(staged, c.want(staged))
            pe.wait_ge(bt_in, c.want(bt_in, 16))
            transposes(BT)
            pe.wait_ge(ct_in, c.want(ct_in, 16))
            g = grp()
            for ch in range(NC):
                ins = mm(piece(g, ch, CH), chunk(BT, ch), chunk(CT, ch))
            ins.then_inc(to_vector[g], c.adds(to_vector[g]))
            for j in range(TILES_PER_GROUP):
                h = 2 * j
                pe.wait_ge(xt_in, c.want(xt_in, 16))
                transposes(XT)
                head()
                if j == 0:
                    pe.wait_ge(btok_ready, c.want(btok_ready))
                for d in range(2):
                    if d == 0:
                        pe.wait_ge(xw_ready, c.want(xw_ready))
                    else:
                        pe.wait_ge(xw1_ready, c.want(xw1_ready))
                    g = grp()
                    for s in range(NSEQ):
                        for k in range(CS - 1):
                            ch = s * CS + (k, CS - 1 - k)[d]
                            ins = mm(piece(g, s * CS + k, P, P), BTOK[:, ch, :], XW[d][:, ch, :])
                    ins.then_inc(to_scalar[g], c.adds(to_scalar[g]))
                if j == 2:
                    pe.wait_ge(y_split, c.want(y_split, 2))
                    out_projection(U0_SSD_OUT)
                head()
                if j == 2:
                    out_projection(U0_SSD_OUT + 1)
                pe.wait_ge(m_ready, c.want(m_ready, 2))
                g = grp()
                for ch in range(NC):
                    for e in range(2):
                        ins = mm(piece(g, ch, CH, SP_, e * SP_), XTOK[:, ch, e * SP_:(e + 1) * SP_],
                                 M[e][0:CH, ch * CH:(ch + 1) * CH])
                ins.then_inc(to_vector[g], c.adds(to_vector[g]))
                for d in range(2):
                    if d == 0:
                        pe.wait_ge(st_ready, c.want(st_ready))
                    g = grp()
                    for ch in range(NC):
                        k = (ch, ch // CS * CS + CS - 1 - ch % CS)[d]
                        ins = mm(piece(g, ch, CH, P), ST[:, d, k, :], chunk(CT, ch))
                    ins.then_inc(to_vector[g], c.adds(to_vector[g]))
            pe.wait_ge(y_split, c.want(y_split, 2))
            out_projection(U0_SSD_OUT + 2)
            out_projection(U0_SSD_OUT + 3)
            assert gb[0] == b

        n = TILES_PER_GROUP
        with pe.Fori(0, GROUPS) as i, \
                c.rounds(GROUPS, i,
                         {staged: 1, bt_in: 16, ct_in: 16, xt_in: 16 * n, v_full: 4 * n, btok_ready: 1,
                          xw_ready: n, xw1_ready: n, m_ready: 2 * n, st_ready: n, y_split: n, w_full[0]: 2,
                          w_full[1]: 2, grp_free[0]: 33, grp_free[1]: 33},
                         {v_used[0]: 2 * n, w_free[0]: 2, w_free[1]: 2, to_scalar[b]: 21, to_scalar[b ^ 1]: 16,
                          to_vector[b]: 12, to_vector[b ^ 1]: 17}):
            scan_round()
        pe.wait_ge(sum_ready, c.want(sum_ready))
        sums_by_token(0, SS, one).then_inc(stat_full, c.adds(stat_full))
        spread_rms(b)
        b ^= 1
        b = feed_forward(U0_FFN1, b)
        pe.wait_ge(sum_ready, c.want(sum_ready))
        sums_by_token(0, SS, one).then_inc(stat_full, c.adds(stat_full))
        spread_rms(b)

    @block.scalar
    def _(act):
        c = Counts()
        sq_by = [None]

        def squares(src, done, dst=SQ):
            if sq_by[0] is not None:
                act.wait_ge(sq_by[0], c.want(sq_by[0]))
            act.activation(dst[:], src, ACT.Square).then_inc(sq_full, c.adds(sq_full))
            sq_by[0] = done

        def gain_and_squares(gain, ready):
            for k in range(KD):
                ready(k)
                act.activation(Uhi[:, k, :], H[:, k, :], ACT.Copy, scale=col(gain, k))\
                    .then_inc(hi_ready, c.adds(hi_ready))
                squares(H[:, k, :], sum_ready if k == KD - 1 else sq_free)

        def take_rms(b):
            act.wait_ge(to_scalar[b], c.want(to_scalar[b]))
            act.activation(banks(RMS[:]), group(b), ACT.Copy).then_inc(act_steps, c.adds(act_steps))
            act.wait_ge(act_steps, c.given(act_steps))
            act.sem_inc(grp_free[b], 1)
            act.sem_inc(rms_ready, 1)

        act.dma_start(cols[:], cols_d).then_inc(const_in, 16)
        act.dma_start(const[:], const_d).then_inc(const_in, 16)
        for k in range(KD):
            act.dma_start(H[:, k, :], x_d[k]).then_inc(x_in[k], 16)
        act.dma_start(trig_k, trig_d[2]).then_inc(trig_in, 16)
        for s in (*w_free, *grp_free):
            act.sem_inc(s, 1)
        act.sem_inc(ov_free, 2)

        act.wait_ge(const_in, c.want(const_in, 16 * 2))
        gain_and_squares("mix0", lambda k: act.wait_ge(x_in[k], c.want(x_in[k], 16)))
        for m in range(KQ + KKV):
            b = m % 2
            act.wait_ge(to_scalar[b], c.want(to_scalar[b]))
            if m >= 2:
                act.wait_ge(u_ready, c.want(u_ready, KD + 1 if m == 2 else 1))
            act.activation(banks(CF[b][:]), group(b), ACT.Copy).then_inc(act_steps, c.adds(act_steps))
            act.wait_ge(act_steps, c.given(act_steps))
            act.sem_inc(grp_free[b], 1)
            gain = col("q_norm", m) if m < KQ else col("kv_norm", m - KQ)
            act.activation(Chi[:, m, :], CF[b][:], ACT.Copy, scale=gain).then_inc(hi_ready, c.adds(hi_ready))
            squares(CF[b][:], sum_ready if m in (KQ - 1, KQ + KKV - 1) else sq_free)
        act.wait_ge(to_scalar[1], c.want(to_scalar[1]))
        act.wait_ge(u_ready, c.want(u_ready))
        act.activation(banks(CF[1][:]), group(1), ACT.Copy).then_inc(act_steps, c.adds(act_steps))
        act.wait_ge(act_steps, c.given(act_steps))
        act.sem_inc(grp_free[1], 1)
        act.wait_ge(sum_ready, c.want(sum_ready))
        act.activation(SQ[:], CF[1][:], ACT.Square).then_inc(rope_sq, c.adds(rope_sq))
        act.wait_ge(to_scalar[0], c.want(to_scalar[0]))
        act.activation(banks(KR[0][NOPE:P, :]), group(0, parts=P - NOPE, at=NOPE), ACT.Copy)\
            .then_inc(act_steps, c.adds(act_steps))
        act.activation(banks(KR[1][0:P - NOPE, :]), group(0, parts=P - NOPE), ACT.Copy)\
            .then_inc(grp_free[0], c.adds(grp_free[0]))
        sq_by[0] = None
        act.wait_ge(stat_full, c.want(stat_full))
        for k in range(2):
            act.dma_start(trig_q[:, k, :], trig_d[k]).then_inc(trig_in, 16)

        steps = [(h, s, t) for h in range(2) for s in range(NSEQ) for t in range(CS)]
        NS = len(steps)

        def attention_round(pair):
            act.wait_ge(to_scalar[0], c.want(to_scalar[0]))
            act.activation(banks(KR[0][0:NOPE, :]), group(0, parts=NOPE), ACT.Copy,
                           scale=col("k_nope")[0:NOPE]).then_inc(act_steps, c.adds(act_steps))
            act.activation(banks(KR[1][NOPE:P, :]), group(0, parts=NOPE, at=NOPE), ACT.Copy,
                           scale=col("k_nope")[NOPE:P]).then_inc(act_steps, c.adds(act_steps))
            act.activation(banks(SQH[2][:]), group(0), ACT.Square).then_inc(act_steps, c.adds(act_steps))
            act.wait_ge(act_steps, c.given(act_steps))
            act.sem_inc(grp_free[0], 1)
            act.sem_inc(k_squared, 1)
            for h, b in ((0, 1), (1, 0)):
                act.wait_ge(to_scalar[b], c.want(to_scalar[b]))
                act.activation(banks(QR[h][:]), group(b), ACT.Copy).then_inc(act_steps, c.adds(act_steps))
                act.wait_ge(act_steps, c.given(act_steps))
                act.sem_inc(grp_free[b], 1)
                act.activation(SQH[h][:], QR[h][:], ACT.Square).then_inc(q_squared, c.adds(q_squared))
            for n in range(NS + 2):
                if n < NS:
                    h, s, t = steps[n]
                    act.wait_ge(nb_ready, c.want(nb_ready))
                    ch = s * CS + t
                    act.activation(
               PR[n % 2][:].rearrange("p (j n) -> p j n", j=2),
               PS[0:CH, 2 * (n % 2):2 * (n % 2) + 2, 0:L // 2], ACT.Exp,
               bias=SMAX[:, n:n + 1], scale=STAT[:, S_QS + h, ch:ch + 1],
               accum_out=SSUM[:, n:n + 1]).then_inc(p_full, c.adds(p_full))
                if n >= 2:
                    h, s, t = steps[n - 2]
                    act.wait_ge(ov_full, c.want(ov_full))
                    act.wait_ge(rinv_ready, c.want(rinv_ready))
                    act.activation(O[:, s * CS + t, h * VD:(h + 1) * VD], PS[0:CH, 6 + n % 2, 0:VD],
                                   ACT.Copy, scale=SINV[:, n - 2:n - 1]).then_inc(ov_free, c.adds(ov_free))
            act.wait_ge(to_scalar[0], c.want(to_scalar[0]))
            act.activation(H[:, bass.ds(pair, 1), :].rearrange("p o (b n) -> p (o b) n", b=NB),
                           group(0), ACT.Copy).then_inc(act_steps, c.adds(act_steps))
            act.wait_ge(act_steps, c.given(act_steps))
            act.sem_inc(grp_free[0], 1)

        with act.Fori(0, PAIRS) as pair, \
                c.rounds(PAIRS, pair,
                         {to_scalar[0]: 3, to_scalar[1]: 1, nb_ready: NS, ov_full: NS, rinv_ready: NS},
                         {act_steps: 6, p_full: NS, ov_free: NS, q_squared: 2}):
            attention_round(pair)

        for k in range(KD):
            act.activation(Ohi[:, k, :], H[:, k, :], ACT.Copy).then_inc(hi_ready, c.adds(hi_ready))
        act.wait_ge(o_split, c.want(o_split, KD))
        act.wait_ge(hi_ready, c.given(hi_ready))
        for k in range(KD):
            act.dma_start(H[:, k, :], x_d[k]).then_inc(x_in[k], 16)
        gain_and_squares("ffn0", lambda k: act.wait_ge(h_ready, c.want(h_ready)))

        def feed_forward(b):
            take_rms(b)

            def silu():
                act.wait_ge(gate_ready, c.want(gate_ready))
                act.activation(SILU[:], GATE[:], ACT.Silu).then_inc(silu_ready, c.adds(silu_ready))

            def split(k):
                act.wait_ge(hid_ready, c.want(hid_ready))
                act.activation(HIDhi[:, k, :], HID[:], ACT.Copy).then_inc(hid_hi, c.adds(hid_hi))

            for k in range(F_STEP):
                silu()
                split(k)
            with act.Fori(0, F_STEPS - 1) as i, \
                    c.rounds(F_STEPS - 1, i,
                             {gate_ready: F_STEP, hid_ready: F_STEP},
                             {silu_ready: F_STEP, hid_hi: F_STEP}):
                for k in range(F_STEP):
                    silu()
                    split(k)

        feed_forward(1)
        gain_and_squares("mix1", lambda k: act.wait_ge(h_ready, c.want(h_ready)))
        act.dma_start(ROWS[:].rearrange("p a d h -> p a (d h)"), rows_d).then_inc(rows_in, 16)
        act.wait_ge(hi_ready, c.given(hi_ready))
        for k in range(KD):
            act.dma_start(scratch_d[D_H + k], H[:, k, :]).then_inc(h_saved, 16)
        for k in range(2):
            act.sem_inc(yc_out[k], 16)
        for s in (*v_used, ss_added):
            act.sem_inc(s, 1)
        act.wait_ge(to_scalar[1], c.want(to_scalar[1]))
        act.activation(banks(XC[0:2 * SHEADS, :]), group(1, parts=2 * SHEADS), ACT.Copy)\
            .then_inc(act_steps, c.adds(act_steps))
        act.wait_ge(act_steps, c.given(act_steps))
        act.sem_inc(grp_free[1], 1)
        act.sem_inc(dt_raw, 1)
        take_rms(0)

        def silu_out(n, to):
            with act.Fori(0, n // 2) as i, \
                    c.rounds(n // 2, i,
                             {yc_ready: 2},
                             {act_steps: 2}):
                for k in range(2):
                    act.wait_ge(yc_ready, c.want(yc_ready))
                    act.activation(YC[k][:], YC[k][:], ACT.Silu).then_inc(act_steps, c.adds(act_steps))
                    act.wait_ge(act_steps, c.given(act_steps))
                    act.dma_start(scratch_d[bass.ds(i * 2 + (to + k), 1)].rearrange("o p t -> p (o t)"), YC[k][:])\
                       .then_inc(yc_out[k], 16)

        silu_out(CONV_TILES, 0)
        act.wait_ge(rows_in, c.want(rows_in, 16))
        act.activation(ROWS[:, 1], ROWS[:, 1], ACT.Exp).then_inc(exp_out, c.adds(exp_out))
        act.wait_ge(exp_in, c.want(exp_in))
        act.activation(E1[:], E1[:], ACT.Exp, scale=-1.0).then_inc(exp_out, c.adds(exp_out))
        silu_out(Z_TILES, D_Z)
        act.wait_ge(exp_in, c.want(exp_in))
        act.activation(WST[:], WST[:], ACT.Exp).then_inc(exp_out, c.adds(exp_out))
        act.activation(DECAY[:], DECAY[:], ACT.Exp).then_inc(exp_out, c.adds(exp_out))

        act.wait_ge(sum_ready, c.want(sum_ready))
        sq_by[0] = None
        for k in range(2):
            act.wait_ge(yc_out[k], 16 * (1 + (CONV_TILES + Z_TILES) // 2))
        act.wait_ge(scan_free, c.want(scan_free))
        for of, to in ((strict_lower, STEPS[0]), (strict_upper, STEPS[1]), (ones_ch, ONES)):
            act.activation(to, of, ACT.Copy).then_inc(act_steps, c.adds(act_steps))
        act.wait_ge(act_steps, c.given(act_steps))
        act.dma_start(XT[:], scratch_d[0]).then_inc(xt_in, 16)
        act.dma_start(BT[:], scratch_d[Z_TILES]).then_inc(bt_in, 16)
        act.dma_start(CT[:], scratch_d[Z_TILES + GROUPS]).then_inc(ct_in, 16)
        act.dma_start(ZT[:], scratch_d[D_Z]).then_inc(zt_in, 16)

        def scan_round(i):
            gb = [B_SCAN]

            def grp():
                gb[0] ^= 1
                return gb[0] ^ 1

            def take(dst, func, width, parts, *also, at=0):
                g = grp()
                act.wait_ge(to_scalar[g], c.want(to_scalar[g]))
                act.activation(dst, group(g, CB * width, parts, at), func).then_inc(act_steps, c.adds(act_steps))
                act.wait_ge(act_steps, c.given(act_steps))
                act.sem_inc(grp_free[g], 1)
                for s in also:
                    act.sem_inc(s, 1)

            def head(e):
                half = slice(e * SP_, (e + 1) * SP_)
                take(banks(EB[0][half, :]), ACT.Exp, CH, SP_, eb_ready, at=e * SP_)
                take(banks(M[e][0:CH, :]), ACT.Exp, CH, CH, l_ready)
                take(banks(EB[1][half, :]), ACT.Exp, CH, SP_, eb_ready, v_used[1], at=e * SP_)

            def finish(j):
                act.wait_ge(y_ready, c.want(y_ready))
                act.activation(Yhi[:, j % 2, :], Y[:], ACT.Copy, scale=NORMG[:, j:j + 1]).then_inc(y_hi, c.adds(y_hi))
                act.wait_ge(ss_added, c.want(ss_added))
                act.activation(SQ[:], Y[:], ACT.Square).then_inc(y_squared, c.adds(y_squared))
                tile_in(ZT, i * TILES_PER_GROUP + (D_Z + j + 1), zt_in)

            def tile_in(dst, index, sem_in):
                act.dma_start(dst[:], scratch_d[bass.ds(index, 1)].rearrange("o p t -> p (o t)")).then_inc(sem_in, 16)

            act.wait_ge(staged, c.want(staged))
            take(BTOK[:].rearrange("p (b c) n -> p b (c n)", b=NB), ACT.Copy, P, CH, btok_ready)
            grp()
            for j in range(TILES_PER_GROUP):
                take(XTOK[:].rearrange("p (b c) n -> p b (c n)", b=NB), ACT.Copy, P, CH, xtok_ready)
                act.wait_ge(eb_free, c.want(eb_free))
                head(0)
                if j:
                    finish(j - 1)
                for d in range(2):
                    g = grp()
                    act.wait_ge(to_scalar[g], c.want(to_scalar[g]))
                    act.activation(ST[:, d].rearrange("p (s k) n -> p s (k n)", s=NSEQ)[:, :, P:],
                                   PS[:, NB * g:NB * g + NB, :].rearrange("p b n -> p (b n)")
                                   .rearrange("p (s n) -> p s n", s=NSEQ)[:, :, 0:(CS - 1) * P],
                                   ACT.Copy).then_inc(act_steps, c.adds(act_steps))
                    act.wait_ge(act_steps, c.given(act_steps))
                    act.sem_inc(grp_free[g], 1)
                    act.sem_inc(st_in, 1)
                head(1)
                if j:
                    act.wait_ge(y_split, c.want(y_split))
                    act.wait_ge(y_squared, c.given(y_squared))
                act.activation(Y[:], XT[:], ACT.Copy, scale=SKIPG[:, j:j + 1]).then_inc(y0_ready, c.adds(y0_ready))
                act.wait_ge(y0_ready, c.given(y0_ready))
                tile_in(XT, i * TILES_PER_GROUP + (j + 1), xt_in)
                gb[0] ^= 1
            finish(TILES_PER_GROUP - 1)
            act.wait_ge(y_split, c.want(y_split))
            act.wait_ge(y_squared, c.given(y_squared))
            tile_in(BT, i + (Z_TILES + 1), bt_in)
            tile_in(CT, i + (Z_TILES + GROUPS + 1), ct_in)

        n = TILES_PER_GROUP
        with act.Fori(0, GROUPS) as i, \
                c.rounds(GROUPS, i,
                         {y_split: n, ss_added: n, staged: 1, to_scalar[B_SCAN]: 21, to_scalar[B_SCAN ^ 1]: 16, y_ready: n,
                          eb_free: n},
                         {act_steps: 1 + 9 * n, y0_ready: n, y_hi: n, y_squared: n}):
            scan_round(i)
        for k in range(2):
            act.dma_start(M[k][:], scratch_d[D_H + k]).then_inc(h_back[k % 2], 16)
        act.wait_ge(sum_ready, c.want(sum_ready))
        for s, n in ((xt_in, Z_TILES), (zt_in, Z_TILES), (bt_in, GROUPS), (ct_in, GROUPS)):
            act.wait_ge(s, 16 * (n + 1))
        take_rms(B_SCAN)

        def mixed(k):
            act.wait_ge(h_ready, c.want(h_ready))
            if k + 2 < KD:
                act.dma_start(M[k % 2][:], scratch_d[D_H + k + 2]).then_inc(h_back[k % 2], 16)

        gain_and_squares("ffn1", mixed)
        feed_forward(B_FFN1)
        for k in range(KD):
            act.wait_ge(h_ready, c.want(h_ready))
            squares(H[:, k, :], sum_ready if k == KD - 1 else sq_free)
        take_rms(B_LAST)
        for k in range(KD):
            act.wait_ge(out_ready, c.want(out_ready))
            act.dma_start(out_d[k], H[:, k, :]).then_inc(out_done, 16)
        act.wait_ge(out_done, 16 * KD)

    @block.vector
    def _(vec):
        c = Counts()

        def add_squares(dst, first, last):
            vec.wait_ge(sq_full, c.want(sq_full))
            if first:
                ins = vec.tensor_copy(dst[:], SQ[:])
            else:
                vec.wait_ge(sq_free, c.given(sq_free))
                ins = vec.tensor_tensor(dst[:], dst[:], SQ[:], ALU.add)
            ins.then_inc(sum_ready if last else sq_free, c.adds(sum_ready if last else sq_free))

        def wait_grp(gb):
            gb[0] ^= 1
            return gb[0] ^ 1

        def lo_part(k, gain, ready=None):
            if ready:
                ready(k)
            vec.wait_ge(hi_ready, c.want(hi_ready))
            vec.scalar_tensor_tensor(Ulo[:, k, :], H[:, k, :], col(gain, k), Uhi[:, k, :].bitcast(F32),
                                     ALU.mult, ALU.subtract).then_inc(u_ready, c.adds(u_ready))
            add_squares(SS, k == 0, k == KD - 1)

        def rsqrt(y, v):
            tmp = STAT[:, S_TMP:S_TMP + 2, :] if len(y.shape) == 3 else stat(S_TMP)
            vec.tensor_scalar(y.bitcast(I32), v.bitcast(I32), 1, None, ALU.logical_shift_right)\
                .then_inc(vec_steps, c.adds(vec_steps))
            vec.wait_ge(vec_steps, c.given(vec_steps))
            vec.tensor_scalar(y.bitcast(I32), y.bitcast(I32), -1.0, float(0x5F3759DF), ALU.mult, ALU.add)\
                .then_inc(vec_steps, c.adds(vec_steps))
            vec.wait_ge(vec_steps, c.given(vec_steps))
            for _ in range(3):
                vec.tensor_tensor(tmp, y, y, ALU.mult).then_inc(vec_steps, c.adds(vec_steps))
                vec.wait_ge(vec_steps, c.given(vec_steps))
                vec.scalar_tensor_tensor(tmp, tmp, -0.5, v, ALU.mult, ALU.mult).then_inc(vec_steps, c.adds(vec_steps))
                vec.wait_ge(vec_steps, c.given(vec_steps))
                vec.scalar_tensor_tensor(y, tmp, 1.5, y, ALU.add, ALU.mult).then_inc(vec_steps, c.adds(vec_steps))
                vec.wait_ge(vec_steps, c.given(vec_steps))

        def stat_sum(k, n=1):
            ap = PS[0:CH, STAT_BANK, k * NC:(k + n) * NC]
            return ap if n == 1 else ap.rearrange("p (k c) -> p k c", c=NC)

        def rms_factor(width):
            vec.wait_ge(stat_full, c.want(stat_full))
            vec.tensor_scalar(stat(S_V), stat_sum(0), 1.0 / width, EPS, ALU.mult, ALU.add)\
                .then_inc(vec_steps, c.adds(vec_steps))
            vec.wait_ge(vec_steps, c.given(vec_steps))
            rsqrt(stat(S_R1), stat(S_V))
            vec.sem_inc(row_ready, 1)

        vec.wait_ge(const_in, c.want(const_in, 16 * 2))
        for k in range(KD):
            lo_part(k, "mix0", lambda k: vec.wait_ge(x_in[k], c.want(x_in[k], 16)))
        for m in range(KQ + KKV):
            vec.wait_ge(hi_ready, c.want(hi_ready))
            gain = col("q_norm", m) if m < KQ else col("kv_norm", m - KQ)
            vec.scalar_tensor_tensor(Clo[:, m, :], CF[m % 2][:], gain, Chi[:, m, :].bitcast(F32),
                                     ALU.mult, ALU.subtract).then_inc(u_ready, c.adds(u_ready))
            add_squares(SSQ[m >= KQ], m in (0, KQ), m in (KQ - 1, KQ + KKV - 1))
        vec.wait_ge(rope_sq, c.want(rope_sq))
        vec.wait_ge(trig_in, c.want(trig_in, 16))
        vec.wait_ge(u_ready, c.given(u_ready))
        vec.scalar_tensor_tensor(seqs(CF[0][:]), seqs(CF[1][:]), col("k_rope"),
                                 trig_k.unsqueeze(1).broadcast_to([P, NSEQ, L]),
                                 ALU.mult, ALU.mult).then_inc(rope_ready, c.adds(rope_ready))
        vec.wait_ge(stat_full, c.want(stat_full))
        vec.tensor_scalar(stat(S_V), stat_sum(0), 1.0 / D_MODEL, EPS, ALU.mult, ALU.add)\
            .then_inc(vec_steps, c.adds(vec_steps))
        vec.wait_ge(vec_steps, c.given(vec_steps))
        rsqrt(stat(S_R1), stat(S_V))
        vec.tensor_tensor(stat(S_R1SQ), stat(S_R1), stat(S_R1), ALU.mult).then_inc(vec_steps, c.adds(vec_steps))
        vec.wait_ge(vec_steps, c.given(vec_steps))
        for k, (rank, dst, dst2) in enumerate(((Q_RANK, S_A, S_A2), (KV_RANK, S_B, S_B2))):
            vec.scalar_tensor_tensor(stat(S_V), stat_sum(1 + k), 1.0 / rank, stat(S_R1SQ), ALU.mult, ALU.mult)\
                .then_inc(vec_steps, c.adds(vec_steps))
            vec.wait_ge(vec_steps, c.given(vec_steps))
            vec.tensor_scalar(stat(S_V), stat(S_V), EPS, None, ALU.add).then_inc(vec_steps, c.adds(vec_steps))
            vec.wait_ge(vec_steps, c.given(vec_steps))
            rsqrt(stat(dst), stat(S_V))
            vec.tensor_tensor(stat(dst), stat(dst), stat(S_R1), ALU.mult).then_inc(vec_steps, c.adds(vec_steps))
            vec.wait_ge(vec_steps, c.given(vec_steps))
            vec.scalar_tensor_tensor(stat(dst2), stat(dst), 1.0 / QK, stat(dst), ALU.mult, ALU.mult)\
                .then_inc(vec_steps, c.adds(vec_steps))
            vec.wait_ge(vec_steps, c.given(vec_steps))
        vec.scalar_tensor_tensor(stat(S_RR), stat_sum(3), 1.0 / QK, stat(S_R1SQ), ALU.mult, ALU.mult)\
            .then_inc(vec_steps, c.adds(vec_steps))
        vec.wait_ge(vec_steps, c.given(vec_steps))
        vec.sem_inc(row_ready, 1)
        vec.tensor_scalar(stat(S_RR), stat(S_RR), EPS, None, ALU.add).then_inc(vec_steps, c.adds(vec_steps))
        vec.wait_ge(vec_steps, c.given(vec_steps))
        vec.wait_ge(trig_in, c.want(trig_in, 32))
        for h in range(2):
            vec.tensor_scalar(trig_q[:, h, :], trig_q[:, h, :], col("q_head", h), None, ALU.mult)\
                .then_inc(vec_steps, c.adds(vec_steps))
            vec.wait_ge(vec_steps, c.given(vec_steps))

        steps = [(h, s, t) for h in range(2) for s in range(NSEQ) for t in range(CS)]
        NS = len(steps)

        def both(k):
            return stat(k).unsqueeze(1).broadcast_to([CH, 2, NC])

        def attention_round():
            v2, y2 = stat(S_V, 2), stat(S_QS, 2)
            vec.wait_ge(stat_full, c.want(stat_full))
            vec.tensor_tensor(v2, stat_sum(2, 2), both(S_B2), ALU.mult).then_inc(vec_steps, c.adds(vec_steps))
            vec.wait_ge(vec_steps, c.given(vec_steps))
            vec.tensor_tensor(v2, v2, both(S_RR), ALU.add).then_inc(vec_steps, c.adds(vec_steps))
            vec.wait_ge(vec_steps, c.given(vec_steps))
            rsqrt(stat(S_KF, 2), v2)
            for h in range(2):
                for part, f in ((0, S_B), (1, S_R1)):
                    vec.tensor_tensor(KS[:, :, 2 * h + (part ^ h)], stat(S_KF + h), stat(f), ALU.mult)\
                        .then_inc(vec_steps, c.adds(vec_steps))
            vec.wait_ge(vec_steps, c.given(vec_steps))
            vec.sem_inc(ks_ready, 1)
            for h in range(2):
                vec.wait_ge(q_squared, c.want(q_squared))
                vec.tensor_tensor(seqs(Q[h][:]), seqs(QR[h][:]),
                                  trig_q[:, h, :].unsqueeze(1).broadcast_to([P, NSEQ, L]), ALU.mult)\
                    .then_inc(q_ready, c.adds(q_ready))
            vec.wait_ge(to_vector[1], c.want(to_vector[1]))
            vec.tensor_tensor(V[:].rearrange("p (b c) d -> p b c d", b=NB),
                             group(1, CB * P, CH).rearrange("p b (c d) -> p b c d", d=P),
                             stat(S_B).rearrange("p (b c) -> p b c", b=NB).unsqueeze(3)
                             .broadcast_to([CH, NB, CB, P]), ALU.mult).then_inc(vec_steps, c.adds(vec_steps))
            vec.wait_ge(vec_steps, c.given(vec_steps))
            vec.sem_inc(grp_free[1], 1)
            vec.sem_inc(v_ready, 1)
            for h in range(2):
                vec.wait_ge(to_vector[h], c.want(to_vector[h]))
                vec.tensor_tensor(banks(KM[h][:]), banks(KR[h][:]), group(h), ALU.mult)\
                    .then_inc(vec_steps, c.adds(vec_steps))
                vec.wait_ge(vec_steps, c.given(vec_steps))
                vec.sem_inc(grp_free[h], 1)
                vec.sem_inc(km_ready, 1)
            vec.wait_ge(stat_full, c.want(stat_full))
            vec.tensor_tensor(v2, stat_sum(0, 2), both(S_A2), ALU.mult).then_inc(vec_steps, c.adds(vec_steps))
            vec.wait_ge(vec_steps, c.given(vec_steps))
            vec.tensor_scalar(v2, v2, EPS, None, ALU.add).then_inc(vec_steps, c.adds(vec_steps))
            vec.wait_ge(vec_steps, c.given(vec_steps))
            rsqrt(y2, v2)
            vec.scalar_tensor_tensor(y2, y2, 1.0 / math.sqrt(QK), both(S_A), ALU.mult, ALU.mult)\
                .then_inc(vec_steps, c.adds(vec_steps))
            vec.wait_ge(vec_steps, c.given(vec_steps))
            for n in range(NS + 1):
                if n < NS:
                    h, s, t = steps[n]
                    ch = s * CS + t
                    vec.wait_ge(sc_full, c.want(sc_full))
                    vec.tensor_reduce(SMAX[:, n:n + 1], PS[0:CH, 2 * (n % 2):2 * (n % 2) + 2, 0:L // 2],
                                      AX_XY, ALU.max).then_inc(vec_steps, c.adds(vec_steps))
                    vec.wait_ge(vec_steps, c.given(vec_steps))
                    vec.tensor_scalar(SMAX[:, n:n + 1], SMAX[:, n:n + 1], STAT[:, S_QS + h, ch:ch + 1],
                                      -1.0, ALU.mult, ALU.mult).then_inc(nb_ready, c.adds(nb_ready))
                if n >= 1:
                    vec.wait_ge(pt_full, c.want(pt_full))
                    vec.tensor_copy(PT[(n - 1) % 2][:].rearrange("p (j k) q -> p j (k q)", j=2),
                                    PS[0:CH, 4:6, 0:L // 2]).then_inc(pt_ready, c.adds(pt_ready))
                    vec.reciprocal(SINV[:, n - 1:n], SSUM[:, n - 1:n]).then_inc(rinv_ready, c.adds(rinv_ready))

        with vec.Fori(0, PAIRS) as i, \
                c.rounds(PAIRS, i,
                         {to_vector[0]: 1, to_vector[1]: 2, stat_full: 2, q_squared: 2, sc_full: NS, pt_full: NS},
                         {vec_steps: 1 + 2 + 11 + 1 + 2 + 11 + 4 + 2 + NS, q_ready: 2, nb_ready: NS,
                          pt_ready: NS, rinv_ready: NS}):
            attention_round()

        for k in range(KD):
            vec.wait_ge(hi_ready, c.want(hi_ready))
            vec.tensor_tensor(Olo[:, k, :], H[:, k, :], Ohi[:, k, :].bitcast(F32), ALU.subtract)\
                .then_inc(o_split, c.adds(o_split))

        def add_to_h(m, b, final):
            vec.wait_ge(to_vector[b], c.want(to_vector[b]))
            ins = vec.tensor_tensor(banks(H[:, m, :]), banks(H[:, m, :]), group(b), ALU.add)
            if final:
                ins.then_inc(vec_steps, c.adds(vec_steps))
                vec.wait_ge(vec_steps, c.given(vec_steps))
                vec.sem_inc(grp_free[b], 1)
                vec.sem_inc(h_ready, 1)
            else:
                ins.then_inc(grp_free[b], c.adds(grp_free[b]))

        for m in range(KD):
            vec.wait_ge(x_in[m], c.want(x_in[m], 16))
            add_to_h(m, m % 2, True)
            lo_part(m, "ffn0")

        def feed_forward(b0, after):
            b = [b0]

            def grp():
                b[0] ^= 1
                return b[0] ^ 1

            def gate(g):
                vec.wait_ge(to_vector[g], c.want(to_vector[g]))
                vec.tensor_tensor(banks(GATE[:]), group(g), banks(RMS[:]), ALU.mult)\
                    .then_inc(vec_steps, c.adds(vec_steps))
                vec.wait_ge(vec_steps, c.given(vec_steps))
                vec.sem_inc(grp_free[g], 1)
                vec.sem_inc(gate_ready, 1)

            def up(g, k):
                vec.wait_ge(to_vector[g], c.want(to_vector[g]))
                vec.tensor_tensor(banks(HID[:]), group(g), banks(RMS[:]), ALU.mult)\
                    .then_inc(vec_steps, c.adds(vec_steps))
                vec.wait_ge(vec_steps, c.given(vec_steps))
                vec.sem_inc(grp_free[g], 1)
                vec.wait_ge(silu_ready, c.want(silu_ready))
                vec.tensor_tensor(HID[:], HID[:], SILU[:], ALU.mult).then_inc(hid_ready, c.adds(hid_ready))
                vec.wait_ge(hid_hi, c.want(hid_hi))
                vec.wait_ge(hid_ready, c.given(hid_ready))
                vec.tensor_tensor(HIDlo[:, k, :], HID[:], HIDhi[:, k, :].bitcast(F32), ALU.subtract)\
                    .then_inc(hid_split, c.adds(hid_split))

            g0 = grp()
            rms_factor(D_MODEL)
            grp()
            vec.wait_ge(rms_ready, c.want(rms_ready))
            gate(g0)
            up(grp(), 0)
            gate(grp())
            up(grp(), 1)
            with vec.Fori(0, F_STEPS - 1) as i, \
                    c.rounds(F_STEPS - 1, i,
                             {to_vector[0]: 6, to_vector[1]: 6, silu_ready: F_STEP, hid_hi: F_STEP},
                             {vec_steps: 2 * F_STEP, hid_ready: F_STEP, hid_split: F_STEP, grp_free[0]: 4,
                              grp_free[1]: 4}):
                gate(grp())
                for m in range(KD):
                    add_to_h(m, grp(), False)
                up(grp(), 0)
                gate(grp())
                up(grp(), 1)
            for m in range(KD):
                add_to_h(m, grp(), True)
                if m:
                    after(m - 1)
            after(KD - 1)
            return b[0]

        b = feed_forward(0, lambda m: lo_part(m, "mix1"))

        rms_factor(D_MODEL)
        vec.wait_ge(to_vector[b], c.want(to_vector[b]))
        for d in range(2):
            ins = vec.tensor_tensor(
                DT[:, d].rearrange("p (b c) h -> p b c h", b=NB),
                group(b, CB * 2 * SHEADS, CH).rearrange("p b (c n) -> p b c n", c=CB)[..., d * SHEADS:(d + 1) * SHEADS],
                stat(S_R1).rearrange("p (b c) -> p b c", b=NB).unsqueeze(3).broadcast_to([CH, NB, CB, SHEADS]),
                ALU.mult)
            if d:
                ins.then_inc(vec_steps, c.adds(vec_steps))
                vec.wait_ge(vec_steps, c.given(vec_steps))
                vec.sem_inc(grp_free[b], 1)
            else:
                ins.then_inc(vec_steps, c.adds(vec_steps))
        vec.wait_ge(rms_ready, c.want(rms_ready))

        def conv(tile, k):
            vec.tensor_copy(TAPS[:], cols[:, bass.ds(tile * (D_CONV + 1) + COLS["conv"], D_CONV + 1)])\
                .then_inc(vec_steps, c.adds(vec_steps))
            vec.wait_ge(vec_steps, c.given(vec_steps))
            x, y, mid = seqs(XC[:]), seqs(YC[k][:]), D_CONV // 2
            vec.tensor_scalar(y, x, TAPS[:, mid:mid + 1], TAPS[:, D_CONV:D_CONV + 1], ALU.mult, ALU.add)\
                .then_inc(vec_steps, c.adds(vec_steps))
            vec.wait_ge(vec_steps, c.given(vec_steps))
            for tap in (0, 1, 3, 4):
                off = tap - mid
                to = slice(max(0, -off), L - max(0, off))
                of = slice(max(0, off), L - max(0, -off))
                ins = vec.scalar_tensor_tensor(y[:, :, to], x[:, :, of], TAPS[:, tap:tap + 1], y[:, :, to],
                                               ALU.mult, ALU.add)
                ins.then_inc(vec_steps, c.adds(vec_steps))
                vec.wait_ge(vec_steps, c.given(vec_steps))
            vec.sem_inc(yc_ready, 1)

        with vec.Fori(0, CONV_TILES // 2) as i, \
                c.rounds(CONV_TILES // 2, i,
                         {to_vector[0]: 1, to_vector[1]: 1, yc_out[0]: 16, yc_out[1]: 16},
                         {vec_steps: 2 * 7}):
            for k, g in ((0, b), (1, b ^ 1)):
                vec.wait_ge(to_vector[g], c.want(to_vector[g]))
                vec.tensor_tensor(banks(XC[:]), group(g), banks(RMS[:]), ALU.mult)\
                    .then_inc(vec_steps, c.adds(vec_steps))
                vec.wait_ge(vec_steps, c.given(vec_steps))
                vec.sem_inc(grp_free[g], 1)
                vec.wait_ge(yc_out[k], c.want(yc_out[k], 16))
                conv(i * 2 + k, k)

        vec.memset(SS[:], 0.0).then_inc(vec_steps, c.adds(vec_steps))

        def z_pair():
            for k, g in ((0, b), (1, b ^ 1)):
                vec.wait_ge(yc_out[k], c.want(yc_out[k], 16))
                vec.wait_ge(to_vector[g], c.want(to_vector[g]))
                vec.tensor_tensor(banks(YC[k][:]), group(g), banks(RMS[:]), ALU.mult)\
                    .then_inc(vec_steps, c.adds(vec_steps))
                vec.wait_ge(vec_steps, c.given(vec_steps))
                vec.sem_inc(grp_free[g], 1)
                vec.sem_inc(yc_ready, 1)

        vec.wait_ge(exp_out, c.want(exp_out))
        vec.tensor_tensor(DT[:], DT[:], ROWS[:, 0].unsqueeze(2).broadcast_to([CH, 2, NC, SHEADS]), ALU.add)\
            .then_inc(vec_steps, c.adds(vec_steps))
        vec.wait_ge(vec_steps, c.given(vec_steps))
        vec.scalar_tensor_tensor(E1[:], DT[:], -1.0, DT[:], ALU.mult, ALU.max).then_inc(exp_in, c.adds(exp_in))
        vec.tensor_scalar(DT[:], DT[:], 0.0, None, ALU.max).then_inc(vec_steps, c.adds(vec_steps))
        vec.wait_ge(vec_steps, c.given(vec_steps))
        vec.wait_ge(exp_out, c.want(exp_out))
        vec.tensor_scalar(E2[:], E1[:], 2.0, None, ALU.add).then_inc(vec_steps, c.adds(vec_steps))
        vec.wait_ge(vec_steps, c.given(vec_steps))
        vec.reciprocal(E2[:], E2[:]).then_inc(vec_steps, c.adds(vec_steps))
        vec.wait_ge(vec_steps, c.given(vec_steps))
        vec.tensor_tensor(E2[:], E1[:], E2[:], ALU.mult).then_inc(vec_steps, c.adds(vec_steps))
        vec.wait_ge(vec_steps, c.given(vec_steps))
        vec.tensor_tensor(E1[:], E2[:], E2[:], ALU.mult).then_inc(vec_steps, c.adds(vec_steps))
        vec.wait_ge(vec_steps, c.given(vec_steps))
        z_pair()
        vec.tensor_scalar(E3[:], E1[:], 1.0 / 15, None, ALU.mult).then_inc(vec_steps, c.adds(vec_steps))
        vec.wait_ge(vec_steps, c.given(vec_steps))
        for k in (13, 11, 9, 7, 5, 3):
            vec.scalar_tensor_tensor(E3[:], E3[:], 1.0 / k, E1[:], ALU.add, ALU.mult)\
                .then_inc(vec_steps, c.adds(vec_steps))
            vec.wait_ge(vec_steps, c.given(vec_steps))
        vec.scalar_tensor_tensor(E3[:], E3[:], 1.0, E2[:], ALU.add, ALU.mult).then_inc(vec_steps, c.adds(vec_steps))
        vec.wait_ge(vec_steps, c.given(vec_steps))
        vec.scalar_tensor_tensor(DT[:], E3[:], 2.0, DT[:], ALU.mult, ALU.add).then_inc(vec_steps, c.adds(vec_steps))
        vec.wait_ge(vec_steps, c.given(vec_steps))
        for d in range(2):
            vec.scalar_tensor_tensor(A[:, d], DT[:, d], -1.0,
                                     ROWS[:, 1, d].unsqueeze(1).broadcast_to([CH, NC, SHEADS]),
                                     ALU.mult, ALU.mult).then_inc(vec_steps, c.adds(vec_steps))
        vec.wait_ge(vec_steps, c.given(vec_steps))
        vec.sem_inc(a_ready, 1)

        with vec.Fori(0, Z_TILES // 2 - 1) as i, \
                c.rounds(Z_TILES // 2 - 1, i,
                         {to_vector[0]: 1, to_vector[1]: 1, yc_out[0]: 16, yc_out[1]: 16},
                         {vec_steps: 2}):
            z_pair()
        vec.wait_ge(to_vector[b], c.want(to_vector[b]))
        vec.tensor_copy(CSUM[:].rearrange("p d c h -> p d (c h)"),
                        PS[0:CH, NB * b:NB * b + 2, 0:NC * SHEADS]).then_inc(vec_steps, c.adds(vec_steps))
        vec.wait_ge(vec_steps, c.given(vec_steps))
        vec.sem_inc(grp_free[b], 1)
        g = b ^ 1
        vec.wait_ge(to_vector[g], c.want(to_vector[g]))
        vec.tensor_copy(DECAY[:].rearrange("p d c h -> p d (c h)"),
                        PS[:, NB * g:NB * g + 2, 0:NC * SHEADS]).then_inc(vec_steps, c.adds(vec_steps))
        vec.wait_ge(vec_steps, c.given(vec_steps))
        vec.sem_inc(grp_free[g], 1)
        vec.sem_inc(scan_free, 1)
        vec.sem_inc(eb_free, 1)
        vec.tensor_tensor(WST[:], DECAY[0:CH], CSUM[:], ALU.subtract).then_inc(exp_in, c.adds(exp_in))
        for k in range(2):
            vec.wait_ge(yc_out[k], c.ahead(yc_out[k], 16))
        vec.wait_ge(exp_in, c.given(exp_in))
        vec.wait_ge(h_cleared, c.want(h_cleared))
        vec.memset(ST[:].rearrange("p d (s k) n -> p (d s) k n", s=NSEQ)[:, :, 0], 0.0)\
            .then_inc(vec_steps, c.adds(vec_steps))
        vec.wait_ge(exp_out, c.want(exp_out, 2))
        vec.tensor_tensor(WST[:], WST[:], DT[:], ALU.mult).then_inc(vec_steps, c.adds(vec_steps))
        vec.wait_ge(vec_steps, c.given(vec_steps))

        def scan_round(i):
            gb = [b]

            def grp():
                gb[0] ^= 1
                vec.wait_ge(to_vector[gb[0] ^ 1], c.want(to_vector[gb[0] ^ 1]))
                return gb[0] ^ 1

            def skip():
                gb[0] ^= 1

            def over(ap, n):
                return ap.unsqueeze(2).broadcast_to([ap.shape[0], NC, n])

            heads = bass.ds(i * HPG, HPG)
            for src, dst in ((A, AHI), (DT, DTG), (WST, WG)):
                vec.tensor_copy(dst[:], src[:, :, :, heads]).then_inc(vec_steps, c.adds(vec_steps))
            vec.tensor_copy(DECG[:, 0], DECAY[:, 0, :, heads]).then_inc(vec_steps, c.adds(vec_steps))
            for k in range(CS):
                vec.tensor_copy(DECG[:, 1].rearrange("p (s k) h -> p s k h", s=NSEQ)[:, :, k],
                                DECAY[:, 1, :, heads].rearrange("p (s k) h -> p s k h", s=NSEQ)[:, :, CS - 1 - k])\
                    .then_inc(vec_steps, c.adds(vec_steps))
            vec.wait_ge(vec_steps, c.given(vec_steps))
            vec.tensor_tensor(ALO[:], A[:, :, :, heads], AHI[:].bitcast(F32), ALU.subtract)\
                .then_inc(vec_steps, c.adds(vec_steps))
            for name, dst in (("skip", SKIPG), ("ssd_norm", NORMG)):
                vec.tensor_copy(dst[:], cols[:, bass.ds(i * TILES_PER_GROUP + COLS[name], TILES_PER_GROUP)])\
                    .then_inc(vec_steps, c.adds(vec_steps))
            vec.wait_ge(vec_steps, c.given(vec_steps))
            vec.sem_inc(staged, 1)
            skip()
            g = grp()
            gv = group(g, CB * CH, CH).rearrange("p b (c t) -> p b c t", t=CH)
            for d, m in ((0, upper), (1, lower)):
                ins = vec.tensor_tensor(G[d][:].rearrange("p (b c) t -> p b c t", b=NB), gv,
                                        m.unsqueeze(1).unsqueeze(1).broadcast_to([CH, NB, CB, CH]), ALU.mult)
                if d:
                    ins.then_inc(vec_steps, c.adds(vec_steps))
                    vec.wait_ge(vec_steps, c.given(vec_steps))
                    vec.sem_inc(grp_free[g], 1)
                else:
                    ins.then_inc(vec_steps, c.adds(vec_steps))
            def low_part(j):
                vec.wait_ge(y_hi, c.want(y_hi))
                vec.scalar_tensor_tensor(Ylo[:, j % 2, :], Y[:], NORMG[:, j:j + 1],
                                         Yhi[:, j % 2, :].bitcast(F32), ALU.mult, ALU.subtract)\
                    .then_inc(y_split, c.adds(y_split))

            def weigh_cb(e):
                t2 = T2[0:CH].rearrange("p (c t) -> p c t", t=CH)
                vec.tensor_tensor(TM, G[0][:], over(dcol(DTG, 0, h + e), CH), ALU.mult)\
                    .then_inc(vec_steps, c.adds(vec_steps))
                vec.tensor_tensor(t2, G[1][:], over(dcol(DTG, 1, h + e), CH), ALU.mult)\
                    .then_inc(vec_steps, c.adds(vec_steps))
                vec.wait_ge(vec_steps, c.given(vec_steps))
                vec.tensor_tensor(TM, TM, t2, ALU.add).then_inc(vec_steps, c.adds(vec_steps))
                vec.wait_ge(vec_steps, c.given(vec_steps))

            def weigh_decays(e):
                m = chunks(M[e][0:CH, :])
                vec.tensor_tensor(m, m, TM, ALU.mult).then_inc(vec_steps, c.adds(vec_steps))
                vec.wait_ge(vec_steps, c.given(vec_steps))
                vec.sem_inc(m_ready, 1)

            for j in range(TILES_PER_GROUP):
                h = 2 * j
                vec.wait_ge(xtok_ready, c.want(xtok_ready))
                vec.tensor_tensor(XW[0][:].rearrange("p c (e n) -> p c e n", e=2),
                                  XTOK[:].rearrange("p c (e n) -> p c e n", e=2),
                                  WG[:, 0, :, h:h + 2].unsqueeze(3).broadcast_to([CH, NC, 2, SP_]),
                                  ALU.mult).then_inc(xw_ready, c.adds(xw_ready))
                weigh_cb(0)
                if j:
                    low_part(j - 1)
                vec.wait_ge(l_ready, c.want(l_ready))
                weigh_decays(0)
                weigh_cb(1)
                gb[0] = b
                vec.wait_ge(st_in, c.want(st_in, 2))
                state = ST[:].rearrange("p d (s k) (e n) -> p (d s) k e n", s=NSEQ, e=2)
                decay = DECG[:].rearrange("p d (s k) h -> p (d s) k h", s=NSEQ)
                carry = T2[:, 0:4 * P].rearrange("p (q e n) -> p q e n", q=2 * NSEQ, e=2)
                for k in range(1, CS - 1):
                    vec.tensor_tensor(carry, state[:, :, k], decay[:, :, k, h:h + 2].unsqueeze(3)
                                      .broadcast_to([P, 2 * NSEQ, 2, SP_]), ALU.mult)\
                        .then_inc(vec_steps, c.adds(vec_steps))
                    vec.wait_ge(vec_steps, c.given(vec_steps))
                    vec.tensor_tensor(state[:, :, k + 1], state[:, :, k + 1], carry, ALU.add)\
                        .then_inc(vec_steps, c.adds(vec_steps))
                    vec.wait_ge(vec_steps, c.given(vec_steps))
                    if j == 2:
                        add_to_h(k - 1, wait_grp(gb), False)
                    if k == (CS - 2 if j == 2 else 2):
                        vec.wait_ge(l_ready, c.want(l_ready))
                        weigh_decays(1)
                vec.sem_inc(st_ready, 1)
                if j == 2:
                    gb[0] = b ^ 1
                    for m in range(KD // 2, KD):
                        add_to_h(m, wait_grp(gb), False)
                gb[0] = b ^ 1
                vec.wait_ge(y0_ready, c.want(y0_ready))
                g = grp()
                vec.tensor_tensor(banks(Y[:]), banks(Y[:]), group(g), ALU.add).then_inc(vec_steps, c.adds(vec_steps))
                vec.wait_ge(vec_steps, c.given(vec_steps))
                vec.sem_inc(grp_free[g], 1)
                vec.wait_ge(eb_ready, c.want(eb_ready, 4))
                for d in range(2):
                    g = grp()
                    vec.tensor_tensor(banks(T2[:]), group(g), banks(EB[d][:]), ALU.mult)\
                        .then_inc(vec_steps, c.adds(vec_steps))
                    vec.wait_ge(vec_steps, c.given(vec_steps))
                    vec.sem_inc(grp_free[g], 1)
                    if d:
                        vec.sem_inc(eb_free, 1)
                    vec.tensor_tensor(Y[:], Y[:], T2[:], ALU.add).then_inc(vec_steps, c.adds(vec_steps))
                    vec.wait_ge(vec_steps, c.given(vec_steps))
                vec.wait_ge(zt_in, c.want(zt_in, 16))
                vec.tensor_tensor(Y[:], Y[:], ZT[:], ALU.mult).then_inc(y_ready, c.adds(y_ready))
            low_part(TILES_PER_GROUP - 1)
            gb[0] = b
            for m in range(KD):
                add_to_h(m, wait_grp(gb), False)
            assert gb[0] == b

        n = TILES_PER_GROUP
        with vec.Fori(0, GROUPS) as i, \
                c.rounds(GROUPS, i,
                         {to_vector[b]: 12, to_vector[b ^ 1]: 17, xtok_ready: n, l_ready: 2 * n, y0_ready: n,
                          eb_ready: 4 * n, st_in: 2 * n, zt_in: 16 * n, y_hi: n},
                         {vec_steps: 9 + CS + 21 * n, grp_free[0]: KD, grp_free[1]: KD, xw_ready: n, y_ready: n,
                          y_split: n}):
            scan_round(i)
        rms_factor(D_INNER)
        vec.wait_ge(rms_ready, c.want(rms_ready))
        for k in range(KD):
            vec.wait_ge(h_back[k % 2], c.want(h_back[k % 2], 16))
            vec.tensor_tensor(H[:, k, :], H[:, k, :], RMS[:], ALU.mult).then_inc(vec_steps, c.adds(vec_steps))
            vec.wait_ge(vec_steps, c.given(vec_steps))
            vec.tensor_tensor(H[:, k, :], H[:, k, :], M[k % 2][:], ALU.add).then_inc(vec_steps, c.adds(vec_steps))
            vec.wait_ge(vec_steps, c.given(vec_steps))
            vec.sem_inc(h_ready, 1)
            if k:
                lo_part(k - 1, "ffn1")
        lo_part(KD - 1, "ffn1")
        b ^= 1
        b = feed_forward(b, lambda m: add_squares(SS, m == 0, m == KD - 1))
        rms_factor(D_MODEL)
        vec.wait_ge(rms_ready, c.want(rms_ready))
        for k in range(KD):
            vec.scalar_tensor_tensor(H[:, k, :], H[:, k, :], col("final", k), RMS[:], ALU.mult, ALU.mult)\
                .then_inc(out_ready, c.adds(out_ready))

    base.close()


def blocks(w, kt_first=True):
    k, m = w.shape
    return w.reshape(k // P, P, m // P, P).transpose(2, 0, 1, 3)


def pad_to(w, m):
    return np.concatenate([w, np.zeros((w.shape[0], m - w.shape[1]), w.dtype)], 1) if w.shape[1] < m else w


def units(b):
    b = b.reshape(-1, BLK, P, P)
    return b.transpose(0, 2, 1, 3).reshape(len(b), P, BLK * P)


def swapped(rope):
    half = ROPE // 2
    return np.concatenate([rope[..., half:], rope[..., :half]], -1)


def head_order(h, v):
    nope, rope = v[..., :NOPE], v[..., NOPE:]
    parts = (nope, rope, swapped(rope)) if h % 2 == 0 else (rope, swapped(rope), nope)
    return np.concatenate(parts, -1)


def ffn_units(gate, up, down):
    g, u = blocks(gate), blocks(up)
    d = blocks(down)
    steps = []
    for i in range(F_STEPS + 1):
        f = slice(i * F_STEP, (i + 1) * F_STEP)
        cols_ = [x for k in range(*f.indices(F_TILES)) for x in (g[k], u[k])] if i < F_STEPS else []
        prev = d[:, (i - 1) * F_STEP:i * F_STEP].reshape(-1, P, P) if i else None
        if not i:
            steps += cols_
        elif cols_:
            steps += [cols_[0], prev, *cols_[1:]]
        else:
            steps += [prev]
    return np.concatenate(steps)


def weight_stream(a):
    w_in = a["mla_w_in"][0]
    rope = w_in[:, Q_RANK + KV_RANK:]
    rope = np.concatenate([rope, swapped(rope)] * 2, 1)
    parts = [blocks(np.concatenate([w_in[:, :Q_RANK + KV_RANK], rope], 1)).reshape(-1, P, P)]
    q_up = a["mla_w_q_up"][0].reshape(Q_RANK, HEADS, QK)
    kv_up = a["mla_w_kv_up"][0].reshape(KV_RANK, HEADS, NOPE + VD)
    for p in range(PAIRS):
        for h in (2 * p, 2 * p + 1):
            parts.append(head_order(h, q_up[:, h]).reshape(KQ, P, P))
        parts.append(kv_up[:, 2 * p:2 * p + 2, :NOPE].reshape(KKV, P, P))
        parts.append(kv_up[:, 2 * p:2 * p + 2, NOPE:].reshape(KKV, P, P))
        parts.append(np.zeros((BLK - KKV, P, P), w_in.dtype))
    parts.append(blocks(a["mla_w_out"][0]).reshape(-1, P, P))
    parts.append(ffn_units(a["ffn_w_gate"][0], a["ffn_w_up"][0], a["ffn_w_down"][0]))
    if U_DT:
        s_in = a["ssd_w_in"][0]
        z, xbc, dt = np.split(s_in, [D_INNER, D_INNER + CONV_TILES * P], 1)
        parts.append(blocks(pad_to(dt, P)).reshape(-1, P, P))
        parts.append(blocks(xbc).reshape(-1, P, P))
        parts.append(blocks(z).reshape(-1, P, P))
        o = blocks(a["ssd_w_out"][0])
        for j in range(0, Z_TILES, 2):
            parts.append(o[:, j:j + 2].reshape(-1, P, P))
    parts.append(ffn_units(a["ffn_w_gate"][1], a["ffn_w_up"][1], a["ffn_w_down"][1]))
    out = units(np.concatenate(parts))
    assert len(out) == UNITS, (len(out), UNITS)
    return out


def column_table(a):
    def by_tile(v):
        return v.reshape(-1, P).T

    k_head = a["mla_k_head_norm"][0]
    kr = k_head[NOPE:]
    conv = np.concatenate([a["ssd_conv_w"][0], a["ssd_conv_b"]], 0)
    conv = conv.reshape(D_CONV + 1, CONV_TILES, P).transpose(2, 1, 0).reshape(P, -1)
    parts = [by_tile(a["mix_norm"][0]), by_tile(a["ffn_norm"][0]), by_tile(a["mix_norm"][1]),
             by_tile(a["ffn_norm"][1]), by_tile(a["final_norm"]), by_tile(a["mla_q_norm"][0]),
             by_tile(a["mla_kv_norm"][0]),
             np.stack([head_order(h, a["mla_q_head_norm"][0]) for h in range(2)], 1),
             np.concatenate([k_head[:NOPE]] * 2)[:, None],
             np.concatenate([kr, swapped(kr)] * 2)[:, None],
             conv, by_tile(np.repeat(a["ssd_d"][0], SP_)), by_tile(a["ssd_norm"][0])]
    table = np.concatenate(parts, 1)
    assert table.shape == (P, NCOLS)
    return np.ascontiguousarray(table)


def constant_table():
    i = np.arange(P)
    c = np.zeros((P, NCONST), np.float32)
    c[:, C_IDENT:C_IDENT + P] = i[:, None] == i
    c[:, C_PAIR:C_PAIR + P] = (i[:, None] // NOPE == i // NOPE) & (i[:, None] % ROPE == i % ROPE)
    c[:, C_UPPER:C_UPPER + P] = i[:, None] <= i
    c[:, C_LOWER:C_LOWER + P] = i[:, None] >= i
    c[:, C_ONES:C_ONES + P] = 1
    c[:, C_STRICT_LOWER:C_STRICT_LOWER + P] = i[:, None] > i
    c[:, C_STRICT_UPPER:C_STRICT_UPPER + P] = i[:, None] < i
    for m, marked in ((M_QE, i < QK), (M_QO, (i < ROPE) | (i >= NOPE)), (M_KE, i < NOPE), (M_KO, i >= NOPE),
                      (M_ROPE, i < ROPE)):
        c[:, C_MASK + m] = marked
    return c


def rotation_tables():
    half = ROPE // 2
    inv_freq = (10000.0 ** (-np.arange(half, dtype=np.float32) / half)).astype(np.float32)
    ang = np.arange(L, dtype=np.float32)[:, None] * inv_freq[None, :]
    cos, sin = np.cos(ang).T, np.sin(ang).T
    turn = np.concatenate([cos, cos, -sin, sin], 0)
    plain = np.ones((NOPE, L), np.float32)
    return np.stack([np.concatenate(x, 0) for x in ((plain, turn), (turn, plain), (turn, turn))]).astype(np.float32)


def kernel(**inputs):
    import concourse.bacc as bacc
    from concourse.bass_utils import run_bass_kernel_spmd

    a = {k: np.asarray(v) for k, v in inputs.items()}
    seqs_ = [np.concatenate([a["meta_tokens"], a[x][0]], 0) for x in ("x_prompt", "x_sample")]
    rows = np.stack([a["ssd_dt_bias"][0].reshape(-1), a["ssd_a_log"][0].reshape(-1)])
    arrays = {
        "x": np.ascontiguousarray(np.concatenate(seqs_, 0).T.reshape(KD, P, T)),
        "w": weight_stream(a),
        "cols": column_table(a),
        "rows": np.ascontiguousarray(np.broadcast_to(rows[None], (CH, 2, 2 * SHEADS))),
        "const": constant_table(),
        "trig": rotation_tables(),
    }
    nc = bacc.Bacc("TRN2", target_bir_lowering=False, num_devices=1)
    tensors = {n: nc.dram_tensor("in_" + n, v.shape, mybir.dt.from_np(v.dtype), kind="ExternalInput").ap()
               for n, v in arrays.items()}
    tensors["out"] = nc.dram_tensor("out", (KD, P, T), F32, kind="ExternalOutput").ap()
    encoder(nc, tensors)
    r = run_bass_kernel_spmd(nc, [{"in_" + n: v for n, v in arrays.items()}], core_ids=[0])
    out = np.asarray(r.results[0]["out"]).reshape(D_MODEL, NSEQ, L)
    return tuple(np.ascontiguousarray(out[:, s, N_META:].T)[None] for s in range(NSEQ))
```
